# Optimizing a Trainium2 kernel written in Bass

```python
import math
import jax
import jax.numpy as jnp
from jax import lax
import numpy as np
import jax, jax.numpy as jnp

D_MODEL = 1024
BATCH = 1
SEQ = 512
DEPTH = 1

DN_HEADS = 4
DN_HEAD_DIM = 128
DN_WIDTH = DN_HEADS * DN_HEAD_DIM
CONV_WIDTH = 4
CHUNK = 64
SWA_HEADS = 8
SWA_KV_HEADS = 2
SWA_GROUP = SWA_HEADS // SWA_KV_HEADS
SWA_HEAD_DIM = 64
SWA_WIDTH = SWA_HEADS * SWA_HEAD_DIM
SWA_KV_WIDTH = SWA_KV_HEADS * SWA_HEAD_DIM
WINDOW = 128
MIX_WIDTH = DN_WIDTH + SWA_WIDTH
IN_SIZES = (3 * DN_WIDTH, DN_WIDTH, DN_HEADS, DN_HEADS, SWA_WIDTH, SWA_KV_WIDTH, SWA_KV_WIDTH)
IN_COLS = sum(IN_SIZES)
N_EXPERTS = 32
TOP_K = 4
D_FF = D_MODEL
SWIGLU_ALPHA = 1.702
SWIGLU_LIMIT = 7.0
MOE_BLOCK = 128
EPS = 1e-6
NEG = -1e30


def _rmsnorm(x, w):
    xf = x.astype(jnp.float32)
    y = xf * lax.rsqrt(jnp.mean(xf * xf, axis=-1, keepdims=True) + EPS)
    return (y * w.astype(jnp.float32)).astype(x.dtype)

def _l2norm(x):
    xf = x.astype(jnp.float32)
    return xf * lax.rsqrt(jnp.sum(xf * xf, axis=-1, keepdims=True) + EPS)

def _causal_conv_silu(u, w):
    n_ch = u.shape[-1]
    y = lax.conv_general_dilated(u, w[:, None, :].astype(u.dtype), window_strides=(1,),
                                 padding=[(CONV_WIDTH - 1, 0)],
                                 dimension_numbers=('NWC', 'WIO', 'NWC'),
                                 feature_group_count=n_ch)
    return jax.nn.silu(y)

def _chunk_gated_delta_rule(q, k, v, g, beta):
    Bn, Sn, H, Dk = q.shape
    Dv = v.shape[-1]
    N = Sn // CHUNK

    def to_chunks(t):
        t = t.astype(jnp.float32).reshape(Bn, N, CHUNK, *t.shape[2:])
        return jnp.moveaxis(t, 3, 2)

    qc = to_chunks(q) * (Dk ** -0.5)
    kc, vc, gc, bc = to_chunks(k), to_chunks(v), to_chunks(g), to_chunks(beta)
    gcum = jnp.cumsum(gc, axis=-1)
    incl = jnp.tril(jnp.ones((CHUNK, CHUNK), bool))
    strict = jnp.tril(jnp.ones((CHUNK, CHUNK), bool), -1)
    diff = gcum[..., :, None] - gcum[..., None, :]
    decay = jnp.where(incl, jnp.exp(jnp.where(incl, diff, 0.0)), 0.0)
    k_beta = kc * bc[..., None]
    a_kk = jnp.where(strict, jnp.einsum('bnhcd,bnhsd->bnhcs', k_beta, kc) * decay, 0.0)
    t_mat = a_kk + jnp.eye(CHUNK, dtype=jnp.float32)
    rhs = jnp.concatenate([vc * bc[..., None], k_beta * jnp.exp(gcum)[..., None]], axis=-1)
    sol = jax.lax.linalg.triangular_solve(t_mat, rhs, left_side=True, lower=True,
                                          unit_diagonal=True)
    u, w = sol[..., :Dv], sol[..., Dv:]
    a_qk = jnp.where(incl, jnp.einsum('bnhcd,bnhsd->bnhcs', qc, kc) * decay, 0.0)
    q_dec = qc * jnp.exp(gcum)[..., None]
    g_last = gcum[..., -1]
    k_dec = kc * jnp.exp(g_last[..., None] - gcum)[..., None]
    chunk_decay = jnp.exp(g_last)
    xs = tuple(jnp.moveaxis(t, 1, 0) for t in (q_dec, k_dec, u, w, a_qk, chunk_decay))

    def step(state, inp):
        q_i, k_i, u_i, w_i, a_i, d_i = inp
        v_new = u_i - jnp.einsum('bhcd,bhde->bhce', w_i, state)
        o_i = (jnp.einsum('bhcd,bhde->bhce', q_i, state)
               + jnp.einsum('bhcs,bhse->bhce', a_i, v_new))
        state = state * d_i[..., None, None] + jnp.einsum('bhcd,bhce->bhde', k_i, v_new)
        return state, o_i

    state0 = jnp.zeros((Bn, H, Dk, Dv), jnp.float32)
    _, o = lax.scan(step, state0, xs)
    return jnp.transpose(o, (1, 0, 3, 2, 4)).reshape(Bn, Sn, H, Dv)

def _sliding_window_attention(q, k, v, q_norm_w, k_norm_w, sinks):
    Bn, Sn, _ = q.shape
    NB = Sn // WINDOW
    q = _rmsnorm(q.reshape(Bn, Sn, SWA_HEADS, SWA_HEAD_DIM), q_norm_w).astype(jnp.float32)
    k = _rmsnorm(k.reshape(Bn, Sn, SWA_KV_HEADS, SWA_HEAD_DIM), k_norm_w).astype(jnp.float32)
    v = v.reshape(Bn, Sn, SWA_KV_HEADS, SWA_HEAD_DIM).astype(jnp.float32)
    pad = jnp.zeros((Bn, WINDOW, SWA_KV_HEADS, SWA_HEAD_DIM), jnp.float32)

    def band(t):
        tp = jnp.concatenate([pad, t], axis=1).reshape(Bn, NB + 1, WINDOW, SWA_KV_HEADS, SWA_HEAD_DIM)
        return jnp.concatenate([tp[:, :-1], tp[:, 1:]], axis=2)

    kw, vw = band(k), band(v)
    qb = q.reshape(Bn, NB, WINDOW, SWA_KV_HEADS, SWA_GROUP, SWA_HEAD_DIM)
    s = jnp.einsum('bnqkgd,bnskd->bnkgqs', qb, kw) * (SWA_HEAD_DIM ** -0.5)
    qi = jnp.arange(WINDOW)[:, None]
    kj = jnp.arange(2 * WINDOW)[None, :]
    rel = (qi + WINDOW - kj).astype(jnp.float32)
    key_pos = jnp.arange(NB)[:, None, None] * WINDOW - WINDOW + kj[None]
    valid = (rel[None] >= 0) & (rel[None] < WINDOW) & (key_pos >= 0)
    slopes = (2.0 ** (-8.0 * jnp.arange(1, SWA_HEADS + 1, dtype=jnp.float32) / SWA_HEADS))
    slopes = slopes.reshape(SWA_KV_HEADS, SWA_GROUP)
    logits = s - slopes[None, None, :, :, None, None] * rel
    logits = jnp.where(valid[None, :, None, None], logits, NEG)
    sink = sinks.astype(jnp.float32).reshape(SWA_KV_HEADS, SWA_GROUP)[None, None, :, :, None]
    m = jnp.maximum(jnp.max(logits, axis=-1), sink)
    p = jnp.exp(logits - m[..., None])
    denom = jnp.sum(p, axis=-1) + jnp.exp(sink - m)
    o = jnp.einsum('bnkgqs,bnskd->bnqkgd', p / denom[..., None], vw)
    return o.reshape(Bn, Sn, SWA_WIDTH)

def _mixer(h, w_in, conv_w, a_log, dt_bias, dn_norm_w, q_norm_w, k_norm_w, sinks, w_out):
    Bn, Sn, _ = h.shape
    proj = h @ w_in
    split_idx = np.cumsum(IN_SIZES)[:-1].tolist()
    dn_qkv, dn_z, dn_a, dn_b, sw_q, sw_k, sw_v = jnp.split(proj, split_idx, axis=-1)
    qkv = _causal_conv_silu(dn_qkv, conv_w)
    q, k, v = jnp.split(qkv, 3, axis=-1)
    q = _l2norm(q.reshape(Bn, Sn, DN_HEADS, DN_HEAD_DIM))
    k = _l2norm(k.reshape(Bn, Sn, DN_HEADS, DN_HEAD_DIM))
    v = v.reshape(Bn, Sn, DN_HEADS, DN_HEAD_DIM)
    beta = jax.nn.sigmoid(dn_b.astype(jnp.float32))
    g = -jnp.exp(a_log.astype(jnp.float32)) * jax.nn.softplus(
        dn_a.astype(jnp.float32) + dt_bias.astype(jnp.float32))
    o_dn = _chunk_gated_delta_rule(q, k, v, g, beta)
    o_dn = _rmsnorm(o_dn, dn_norm_w) * jax.nn.silu(
        dn_z.reshape(Bn, Sn, DN_HEADS, DN_HEAD_DIM).astype(jnp.float32))
    o_dn = o_dn.reshape(Bn, Sn, DN_WIDTH)
    o_sw = _sliding_window_attention(sw_q, sw_k, sw_v, q_norm_w, k_norm_w, sinks)
    mixed = jnp.concatenate([o_dn.astype(h.dtype), o_sw.astype(h.dtype)], axis=-1)
    return mixed @ w_out

def _moe(h, w_router, b_router, w_up, b_up, w_down, b_down):
    Bn, Sn, D = h.shape
    T = Bn * Sn
    xf = h.reshape(T, D)
    logits = (xf @ w_router).astype(jnp.float32) + b_router.astype(jnp.float32)
    top_val, top_idx = lax.top_k(logits, TOP_K)
    gates = jax.nn.softmax(top_val, axis=-1)
    n_assign = T * TOP_K
    flat_e = top_idx.reshape(-1)
    flat_tok = jnp.arange(n_assign, dtype=jnp.int32) // TOP_K
    flat_gate = gates.reshape(-1)
    order = jnp.argsort(flat_e)
    se, stok, sgate = flat_e[order], flat_tok[order], flat_gate[order]
    counts = jnp.bincount(flat_e, length=N_EXPERTS)
    padded = (counts + MOE_BLOCK - 1) // MOE_BLOCK * MOE_BLOCK
    start = jnp.cumsum(counts) - counts
    pend = jnp.cumsum(padded)
    pstart = pend - padded
    dest = pstart[se] + (jnp.arange(n_assign) - start[se])
    n_pad = n_assign + N_EXPERTS * MOE_BLOCK
    n_blocks = n_pad // MOE_BLOCK
    row_tok = jnp.zeros((n_pad,), jnp.int32).at[dest].set(stok)
    row_gate = jnp.zeros((n_pad,), jnp.float32).at[dest].set(sgate)
    block_e = jnp.minimum(jnp.searchsorted(pend, jnp.arange(n_blocks) * MOE_BLOCK, side='right'),
                          N_EXPERTS - 1)
    xs = xf[row_tok].reshape(n_blocks, MOE_BLOCK, D)

    def expert_block(args):
        xb, e = args
        hu = xb @ w_up[e] + b_up[e]
        x_glu = jnp.minimum(hu[:, :D_FF], SWIGLU_LIMIT)
        x_lin = jnp.clip(hu[:, D_FF:], -SWIGLU_LIMIT, SWIGLU_LIMIT)
        act = x_glu * jax.nn.sigmoid(SWIGLU_ALPHA * x_glu) * (x_lin + 1.0)
        return act @ w_down[e] + b_down[e]

    ys = lax.map(expert_block, (xs, block_e)).reshape(n_pad, D)
    ys = ys.astype(jnp.float32) * row_gate[:, None]
    out = jax.ops.segment_sum(ys, row_tok, num_segments=T)
    return out.reshape(Bn, Sn, D).astype(h.dtype)

def first_inputs(seed: int = 0) -> dict:
    key = jax.random.key(seed)
    ks = jax.random.split(key, 24)
    L = DEPTH

    def nrm(k, shape, scale):
        return jax.random.normal(k, shape, jnp.float32) * scale

    dt = jnp.exp(jax.random.uniform(ks[8], (L, DN_HEADS), jnp.float32,
                                    math.log(1e-3), math.log(1e-1)))
    return {
        'x': nrm(ks[0], (BATCH, SEQ, D_MODEL), 1.0),
        'c': nrm(ks[1], (BATCH, D_MODEL), 1.0),
        'w_ada': nrm(ks[2], (L, D_MODEL, 6 * D_MODEL), 0.5 * D_MODEL ** -0.5),
        'b_ada': nrm(ks[3], (L, 6 * D_MODEL), 0.02),
        'norm1_w': 1.0 + nrm(ks[4], (L, D_MODEL), 0.02),
        'w_in': nrm(ks[5], (L, D_MODEL, IN_COLS), D_MODEL ** -0.5),
        'conv_w': nrm(ks[6], (L, CONV_WIDTH, 3 * DN_WIDTH), CONV_WIDTH ** -0.5),
        'a_log': jnp.log(jax.random.uniform(ks[7], (L, DN_HEADS), jnp.float32, 1.0, 16.0)),
        'dt_bias': dt + jnp.log(-jnp.expm1(-dt)),
        'dn_norm_w': 1.0 + nrm(ks[9], (L, DN_HEAD_DIM), 0.02),
        'q_norm_w': 1.0 + nrm(ks[10], (L, SWA_HEAD_DIM), 0.02),
        'k_norm_w': 1.0 + nrm(ks[11], (L, SWA_HEAD_DIM), 0.02),
        'sinks': nrm(ks[12], (L, SWA_HEADS), 1.0),
        'w_out': nrm(ks[13], (L, MIX_WIDTH, D_MODEL), MIX_WIDTH ** -0.5),
        'norm2_w': 1.0 + nrm(ks[14], (L, D_MODEL), 0.02),
        'w_router': nrm(ks[15], (L, D_MODEL, N_EXPERTS), D_MODEL ** -0.5),
        'b_router': nrm(ks[16], (L, N_EXPERTS), 0.01),
        'w_up': nrm(ks[17], (L, N_EXPERTS, D_MODEL, 2 * D_FF), D_MODEL ** -0.5),
        'b_up': nrm(ks[18], (L, N_EXPERTS, 2 * D_FF), 0.01),
        'w_down': nrm(ks[19], (L, N_EXPERTS, D_FF, D_MODEL), D_FF ** -0.5),
        'b_down': nrm(ks[20], (L, N_EXPERTS, D_MODEL), 0.01),
    }

def first_block(x, c, w_ada, b_ada, norm1_w, w_in, conv_w, a_log, dt_bias, dn_norm_w,
              q_norm_w, k_norm_w, sinks, w_out, norm2_w, w_router, b_router,
              w_up, b_up, w_down, b_down):
    out_dtype = x.dtype
    c_act = jax.nn.silu(c)
    for l in range(DEPTH):
        mod = (c_act @ w_ada[l] + b_ada[l])[:, None, :]
        shift1, scale1, gate1, shift2, scale2, gate2 = jnp.split(mod, 6, axis=-1)
        h = _rmsnorm(x, norm1_w[l]) * (1.0 + scale1) + shift1
        y = _mixer(h, w_in[l], conv_w[l], a_log[l], dt_bias[l], dn_norm_w[l],
                   q_norm_w[l], k_norm_w[l], sinks[l], w_out[l])
        x = x + gate1 * y
        h = _rmsnorm(x, norm2_w[l]) * (1.0 + scale2) + shift2
        x = x + gate2 * _moe(h, w_router[l], b_router[l], w_up[l], b_up[l], w_down[l], b_down[l])
    return x.astype(out_dtype)


DEPTH_2 = 2

N_MIXERS = 2
N_Q_HEADS = 8
N_KV_HEADS = 2
HEAD_DIM = D_MODEL // N_Q_HEADS
Q_PER_KV = N_Q_HEADS // N_KV_HEADS
ROT_DIM = HEAD_DIM // 4
ROPE_THETA = 500000.0
BLOCK = 128
D_RNN = 3 * D_MODEL // 2
N_RNN_BLOCKS = 16
RNN_BLOCK_W = D_RNN // N_RNN_BLOCKS
CONV_W = 4
CONV_LEFT = 2
LRU_C = 8.0
D_FF_2 = 4 * D_MODEL
DN_ALPHA = (2.0 * DEPTH_2) ** 0.25
DN_BETA = (8.0 * DEPTH_2) ** -0.25
LN_EPS = 1e-5
ADA_INIT = 0.5

N_ATTN_LAYERS = (DEPTH_2 + N_MIXERS - 1) // N_MIXERS
N_RNN_LAYERS = DEPTH_2 // N_MIXERS


def layer_norm(x, g, b):
    xf = x.astype(jnp.float32)
    mu = jnp.mean(xf, axis=-1, keepdims=True)
    var = jnp.mean(jnp.square(xf - mu), axis=-1, keepdims=True)
    y = (xf - mu) * lax.rsqrt(var + LN_EPS)
    return (y * g.astype(jnp.float32) + b.astype(jnp.float32)).astype(x.dtype)

def ada_modulation(c, w, b):
    mod = jax.nn.silu(c) @ w + b
    shift, scale, gate = jnp.split(mod, 3, axis=-1)
    return shift[:, None, :], scale[:, None, :], gate[:, None, :]

def partial_rope(t, cos, sin):
    half = ROT_DIM // 2
    tr = t[..., :ROT_DIM].astype(jnp.float32)
    t1, t2 = tr[..., :half], tr[..., half:]
    cs, sn = cos[None, :, None, :], sin[None, :, None, :]
    rot = jnp.concatenate([t1 * cs - t2 * sn, t2 * cs + t1 * sn], axis=-1).astype(t.dtype)
    return jnp.concatenate([rot, t[..., ROT_DIM:]], axis=-1)

def windowed_gqa(h, w_in, w_out, sinks):
    B, S, _ = h.shape
    nblk = S // BLOCK
    qkv = h @ w_in
    q, k, v = jnp.split(qkv, [N_Q_HEADS * HEAD_DIM, (N_Q_HEADS + N_KV_HEADS) * HEAD_DIM], axis=-1)
    q = q.reshape(B, S, N_Q_HEADS, HEAD_DIM)
    k = k.reshape(B, S, N_KV_HEADS, HEAD_DIM)
    v = v.reshape(B, S, N_KV_HEADS, HEAD_DIM)
    pos = jnp.arange(S, dtype=jnp.float32)
    inv_freq = ROPE_THETA ** (-jnp.arange(0, ROT_DIM, 2, dtype=jnp.float32) / ROT_DIM)
    ang = pos[:, None] * inv_freq[None, :]
    cos, sin = jnp.cos(ang), jnp.sin(ang)
    q = partial_rope(q, cos, sin)
    k = partial_rope(k, cos, sin)
    qb = q.reshape(B, nblk, BLOCK, N_KV_HEADS, Q_PER_KV, HEAD_DIM)

    def band(t):
        tp = jnp.pad(t, ((0, 0), (BLOCK, BLOCK), (0, 0), (0, 0)))
        tb = tp.reshape(B, nblk + 2, BLOCK, N_KV_HEADS, HEAD_DIM)
        return jnp.concatenate([tb[:, :-2], tb[:, 1:-1], tb[:, 2:]], axis=2)

    kb, vb = band(k), band(v)
    scores = jnp.einsum("bnqhgd,bnjhd->bnhgqj", qb, kb,
                        preferred_element_type=jnp.float32) * (HEAD_DIM ** -0.5)
    blk = jnp.arange(nblk)[:, None, None] * BLOCK
    qpos = blk + jnp.arange(BLOCK)[None, :, None]
    kpos = blk - BLOCK + jnp.arange(3 * BLOCK)[None, None, :]
    valid = (jnp.abs(qpos - kpos) <= WINDOW) & (kpos >= 0) & (kpos < S)
    scores = jnp.where(valid[None, :, None, None], scores, -jnp.inf)
    sink = sinks.astype(jnp.float32).reshape(N_KV_HEADS, Q_PER_KV)[None, None, :, :, None, None]
    m = jnp.maximum(jnp.max(scores, axis=-1, keepdims=True), sink)
    p = jnp.exp(scores - m)
    denom = jnp.sum(p, axis=-1, keepdims=True) + jnp.exp(sink - m)
    probs = (p / denom).astype(v.dtype)
    o = jnp.einsum("bnhgqj,bnjhd->bnqhgd", probs, vb)
    o = o.reshape(B, S, N_Q_HEADS * HEAD_DIM)
    return o @ w_out

def centred_depthwise_conv(x, w, b):
    S = x.shape[1]
    xp = jnp.pad(x, ((0, 0), (CONV_LEFT, CONV_W - 1 - CONV_LEFT), (0, 0)))
    out = xp[:, 0:S] * w[0] + b
    for j in range(1, CONV_W):
        out = out + xp[:, j:j + S] * w[j]
    return out

def rg_lru(x, w_a, b_a, w_x, b_x, lam, reverse):
    B, S, _ = x.shape
    xb = x.reshape(B, S, N_RNN_BLOCKS, RNN_BLOCK_W)
    r = jax.nn.sigmoid((jnp.einsum("bsni,nij->bsnj", xb, w_a).reshape(B, S, D_RNN) + b_a).astype(jnp.float32))
    i = jax.nn.sigmoid((jnp.einsum("bsni,nij->bsnj", xb, w_x).reshape(B, S, D_RNN) + b_x).astype(jnp.float32))
    log_a = -LRU_C * r * jax.nn.softplus(-lam.astype(jnp.float32))
    a = jnp.exp(log_a)
    mult = jnp.sqrt(-jnp.expm1(2.0 * log_a))
    u = mult * (i * x.astype(jnp.float32))

    def combine(left, right):
        a_l, b_l = left
        a_r, b_r = right
        return a_l * a_r, a_r * b_l + b_r

    _, hs = lax.associative_scan(combine, (a, u), axis=1, reverse=reverse)
    return hs

def recurrent_block(h, w_in, conv_w, conv_b, w_a, b_a, w_x, b_x, lam, w_out):
    z = h @ w_in
    xr, gate = jnp.split(z, 2, axis=-1)
    xr = centred_depthwise_conv(xr, conv_w, conv_b)
    y = (rg_lru(xr, w_a[0], b_a[0], w_x[0], b_x[0], lam[0], reverse=False)
         + rg_lru(xr, w_a[1], b_a[1], w_x[1], b_x[1], lam[1], reverse=True))
    y = y.astype(h.dtype) * jax.nn.gelu(gate)
    return y @ w_out

def sq_relu_mlp(h, w1, w2):
    return jnp.square(jax.nn.relu(h @ w1)) @ w2

def second_inputs(seed: int = 0) -> dict:
    key = jax.random.key(seed)
    ks = jax.random.split(key, 24)
    nrm = lambda k, shape, s: jax.random.normal(k, shape, jnp.float32) * s
    u = jax.random.uniform(ks[17], (N_RNN_LAYERS, 2, D_RNN), jnp.float32, 0.9, 0.999)
    s_lam = u ** (1.0 / LRU_C)
    lam = jnp.log(s_lam) - jnp.log1p(-s_lam)
    return {
        "x": nrm(ks[0], (BATCH, SEQ, D_MODEL), 1.0),
        "c": nrm(ks[1], (BATCH, D_MODEL), 1.0),
        "ada_w": nrm(ks[2], (DEPTH_2, 2, D_MODEL, 3 * D_MODEL), ADA_INIT * D_MODEL ** -0.5),
        "ada_b": nrm(ks[3], (DEPTH_2, 2, 3 * D_MODEL), 0.01),
        "ln_g": 1.0 + nrm(ks[4], (DEPTH_2, 2, D_MODEL), 0.02),
        "ln_b": nrm(ks[5], (DEPTH_2, 2, D_MODEL), 0.02),
        "attn_w_in": nrm(ks[6], (N_ATTN_LAYERS, D_MODEL, (N_Q_HEADS + 2 * N_KV_HEADS) * HEAD_DIM), D_MODEL ** -0.5),
        "attn_w_out": nrm(ks[7], (N_ATTN_LAYERS, N_Q_HEADS * HEAD_DIM, D_MODEL), DN_BETA * (N_Q_HEADS * HEAD_DIM) ** -0.5),
        "attn_sinks": nrm(ks[8], (N_ATTN_LAYERS, N_Q_HEADS), 1.0),
        "rnn_w_in": nrm(ks[9], (N_RNN_LAYERS, D_MODEL, 2 * D_RNN), D_MODEL ** -0.5),
        "rnn_conv_w": nrm(ks[10], (N_RNN_LAYERS, CONV_W, D_RNN), CONV_W ** -0.5),
        "rnn_conv_b": nrm(ks[11], (N_RNN_LAYERS, D_RNN), 0.01),
        "rnn_w_a": nrm(ks[12], (N_RNN_LAYERS, 2, N_RNN_BLOCKS, RNN_BLOCK_W, RNN_BLOCK_W), RNN_BLOCK_W ** -0.5),
        "rnn_b_a": nrm(ks[13], (N_RNN_LAYERS, 2, D_RNN), 0.01),
        "rnn_w_x": nrm(ks[14], (N_RNN_LAYERS, 2, N_RNN_BLOCKS, RNN_BLOCK_W, RNN_BLOCK_W), RNN_BLOCK_W ** -0.5),
        "rnn_b_x": nrm(ks[15], (N_RNN_LAYERS, 2, D_RNN), 0.01),
        "rnn_lam": lam,
        "rnn_w_out": nrm(ks[16], (N_RNN_LAYERS, D_RNN, D_MODEL), DN_BETA * D_RNN ** -0.5),
        "mlp_w1": nrm(ks[18], (DEPTH_2, D_MODEL, D_FF_2), D_MODEL ** -0.5),
        "mlp_w2": nrm(ks[19], (DEPTH_2, D_FF_2, D_MODEL), DN_BETA * D_FF_2 ** -0.5),
    }

def second_block(x, c, ada_w, ada_b, ln_g, ln_b, attn_w_in, attn_w_out, attn_sinks,
              rnn_w_in, rnn_conv_w, rnn_conv_b, rnn_w_a, rnn_b_a, rnn_w_x, rnn_b_x, rnn_lam,
              rnn_w_out, mlp_w1, mlp_w2):
    for i in range(DEPTH_2):
        j = i // N_MIXERS
        shift, scale, gate = ada_modulation(c, ada_w[i, 0], ada_b[i, 0])
        h = x * (1.0 + scale) + shift
        if i % N_MIXERS == 0:
            y = windowed_gqa(h, attn_w_in[j], attn_w_out[j], attn_sinks[j])
        else:
            y = recurrent_block(h, rnn_w_in[j], rnn_conv_w[j], rnn_conv_b[j], rnn_w_a[j], rnn_b_a[j],
                                rnn_w_x[j], rnn_b_x[j], rnn_lam[j], rnn_w_out[j])
        x = layer_norm(DN_ALPHA * x + (1.0 + gate) * y, ln_g[i, 0], ln_b[i, 0])
        shift, scale, gate = ada_modulation(c, ada_w[i, 1], ada_b[i, 1])
        y = sq_relu_mlp(x * (1.0 + scale) + shift, mlp_w1[i], mlp_w2[i])
        x = layer_norm(DN_ALPHA * x + (1.0 + gate) * y, ln_g[i, 1], ln_b[i, 1])
    return x


def setup_inputs(seed=0):
    out = dict(first_inputs(seed))
    for name, value in second_inputs(seed + 1).items():
        if name != "x":
            out[name + "_2"] = value
    return out


def reference(
    x, c, w_ada, b_ada, norm1_w, w_in, conv_w, a_log, dt_bias, dn_norm_w, q_norm_w, k_norm_w,
    sinks, w_out, norm2_w, w_router, b_router, w_up, b_up, w_down, b_down, c_2, ada_w_2,
    ada_b_2, ln_g_2, ln_b_2, attn_w_in_2, attn_w_out_2, attn_sinks_2, rnn_w_in_2, rnn_conv_w_2,
    rnn_conv_b_2, rnn_w_a_2, rnn_b_a_2, rnn_w_x_2, rnn_b_x_2, rnn_lam_2, rnn_w_out_2, mlp_w1_2,
    mlp_w2_2,
):
    x = first_block(
        x, c, w_ada, b_ada, norm1_w, w_in, conv_w, a_log, dt_bias, dn_norm_w, q_norm_w,
        k_norm_w, sinks, w_out, norm2_w, w_router, b_router, w_up, b_up, w_down, b_down,
    )
    return second_block(
        x, c_2, ada_w_2, ada_b_2, ln_g_2, ln_b_2, attn_w_in_2, attn_w_out_2, attn_sinks_2,
        rnn_w_in_2, rnn_conv_w_2, rnn_conv_b_2, rnn_w_a_2, rnn_b_a_2, rnn_w_x_2, rnn_b_x_2,
        rnn_lam_2, rnn_w_out_2, mlp_w1_2, mlp_w2_2,
    )


_drawn_inputs = setup_inputs


def setup_inputs(seed=0):
    import zlib

    import numpy as np

    out = dict(_drawn_inputs(seed))
    spreads = {}
    factors = {'norm1_w': 4.923,
     'dn_norm_w': 6.085,
     'q_norm_w': 8.0,
     'k_norm_w': 8.0,
     'sinks': 102.767,
     'norm2_w': 3.078,
     'b_router': 3.99,
     'b_up': 8.0,
     'b_down': 48.4,
     'attn_sinks_2': 64.0,
     'rnn_conv_b_2': 3.176,
     'rnn_b_a_2': 59.2,
     'rnn_b_x_2': 23.728}
    for name, (base, spread) in spreads.items():
        noise = np.random.default_rng([zlib.crc32(name.encode()), seed]).standard_normal(out[name].shape)
        drawn = base * np.exp(spread * noise) if base else spread * noise
        out[name] = jnp.asarray(drawn.astype(out[name].dtype))
    for name, factor in factors.items():
        out[name] = (out[name] * factor).astype(out[name].dtype)
    return out
```

```python
from contextlib import ExitStack

import numpy as np
import concourse.bass as bass
from concourse import mybir

ALU = mybir.AluOpType
ACT = mybir.ActivationFunctionType
AX_X = mybir.AxisListType.X
F32 = mybir.dt.float32
BF16 = mybir.dt.bfloat16
I32 = mybir.dt.int32
U32 = mybir.dt.uint32

P = 128
T = 512
TT = T // P
D = 1024
KT = D // P
CH = 512
DH, DD = 4, 128
C = 64
NC = T // C
NS = DH * NC
SH, SG, SD = 8, 2, 64
SQ = SH // SG
E, TOPK = 32, 4
BLK = 128
MAXB = 48
LROWS = E * T + 17 * BLK
DUMMY = T * TOPK * 2
ALPHA, LIMIT = 1.702, 7.0
EPS, NEG = 1e-6, -1e30
QH, KH, HD = 8, 2, 128
QK = QH // KH
ROT = HD // 4
RW, RB = 96, 16
LRU_C = 8.0
LN_EPS = 1e-5
DN_ALPHA = 4.0 ** 0.25


def constants():
    k = {}
    k["ident"] = np.eye(P, dtype=np.float32)
    r = np.arange(P)
    k["upper"] = (r[:, None] <= r[None, :]).astype(np.float32)
    k["upstrict"] = (r[:, None] < r[None, :]).astype(np.float32)
    k["lowstrict"] = (r[:, None] > r[None, :]).astype(np.float32)
    kj = np.arange(2 * P)[None, :]
    rel = (r[:, None] + P - kj).astype(np.float32)
    slopes = 2.0 ** (-8.0 * np.arange(1, SH + 1, dtype=np.float32) / SH)
    valid = (rel >= 0) & (rel < P)
    tab = np.where(valid[:, None, :], -slopes[None, :, None] * rel[:, None, :], NEG).astype(np.float32)
    k["swbias"] = np.ascontiguousarray(tab.reshape(P, SH * 2 * P))
    m = np.zeros((P, TT, 3 * P), np.float32)
    kj = np.arange(3 * P)[None, :]
    for b in range(TT):
        kpos = b * P - P + kj
        ok = (np.abs(r[:, None] + P - kj) <= P) & (kpos >= 0) & (kpos < T)
        m[:, b] = np.where(ok, 0.0, NEG)
    k["gqbias"] = m.reshape(P, TT * 3 * P)
    inv = 500000.0 ** (-np.arange(0, ROT, 2, dtype=np.float32) / ROT)
    ang = (np.arange(T, dtype=np.float32)[:, None] * inv[None, :].astype(np.float32)).astype(np.float32)
    cs = np.stack([np.cos(ang), np.sin(ang)], 0).astype(np.float32)
    k["rope"] = np.ascontiguousarray(cs.reshape(2, TT, P, ROT // 2).transpose(2, 1, 0, 3)).reshape(P, -1)
    k["iota32"] = np.broadcast_to(np.arange(E, dtype=np.float32), (P, E)).copy()
    tok = np.arange(TT)[None, :, None] * P + r[:, None, None]
    pairs = np.stack([np.broadcast_to(tok, (P, TT, TOPK)), tok * TOPK + np.arange(TOPK)[None, None, :]], -1)
    k["pairs"] = np.ascontiguousarray(pairs.astype(np.int32).reshape(P, -1))
    k["pmod"] = (r % E).astype(np.float32)[:, None].copy()
    return k


def build(nc, A, out, dbg=None):
    ctx = ExitStack()
    sems = {}

    def S(name):
        if name not in sems:
            sems[name] = ctx.enter_context(nc.semaphore(name))
        return sems[name]

    with ctx:
        ctx.enter_context(nc.allow_non_contiguous_dma(reason="small vectors laid along the partitions"))
        def sb(name, shape, dt=F32):
            return ctx.enter_context(nc.sbuf_tensor(name, shape, dt))

        def dram(name, shape, dt=F32):
            return nc.dram_tensor(name, shape, dt, kind="Internal").ap()

        X = sb("X", [P, TT, D])
        hT = sb("hT", [P, KT, T])
        slots = sb("slots", [P, 6, KT, CH])
        work = sb("work", [P, 13312])
        stage = sb("stage", [P, D])
        tmp = sb("tmp", [P, D])
        modA = sb("modA", [P, D])
        modB = sb("modB", [P, D])
        modG = sb("modG", [P, D])
        ident = sb("ident", [P, P])
        upper = sb("upper", [P, P])
        upstrict = sb("upstrict", [P, P])
        lowstrict = sb("lowstrict", [P, P])
        ones = sb("ones", [P, P])
        small = sb("small", [P, 256])
        cT = sb("cT", [P, 2, KT])
        epsc = sb("epsc", [P, 2])
        mod_dram = dram("mod_dram", (1, 6 * D + 4 * 3 * D))
        ps = ctx.enter_context(nc.psum_tensor("ps", [P, 8, CH], F32))
        scratch = slots[:, 2:6].rearrange("p s k n -> p (s k n)")

        def wview(a, r=P):
            return a.rearrange("(t p) n -> p t n", p=r)

        landed = [S(f"landed{i}") for i in range(6)]
        freed = [S(f"freed{i}") for i in range(6)]
        loads = [0] * 6
        uses = [0] * 6

        def load(sp, s, src, dst=None):
            sp.wait_ge(freed[s], loads[s] + 1)
            sp.dma_start(slots[:, s] if dst is None else dst, src).then_inc(landed[s], 16)
            loads[s] += 1

        def take(eng, s):
            eng.wait_ge(landed[s], 16 * (uses[s] + 1))
            uses[s] += 1

        ORDER = {"1": 0, "w": 1, "2": 2, "3": 3, "o": 4, "4": 5, "5": 6, "6": 7}
        PER_USE = {"stage_free": TT + 1, "stage_ready": TT, "turned_out": TT + 1}
        OTHER = {
            "mod_in": {"1": 0, "2": 64, "3": 128, "4": 176, "5": 224, "6": 272},
            "var": {"1": 0, "dn": 1, "2": 2, "a": 3, "b": 4, "c": 5, "d": 6},
            "sd": {"1": 0, "dn": 1, "2": 2, "a": 3, "b": 4, "c": 5, "d": 6},
            "bank_free": {"q": 0, "w": 16, "at": 28, "o": 44, "r": 56, "_ro": 76},
            "product": {"q": 0, "w": 24, "at": 32, "o": 44, "r": 52, "_ro": 84},
            "ln_in": {"a": 0, "b": 32, "c": 64, "d": 96},
            "hid_free": {"m0": 0, "m1": 36}, "hid": {"m0": 0, "m1": 32}, "hid_sq": {"m0": 0, "m1": 32},
            "relu_free": {"m0": 0, "m1": 34}, "out_free": {"m0": 0, "m1": 36}, "outp": {"m0": 0, "m1": 32},
        }

        def before(name, key):
            return OTHER[name][key] if name in OTHER else PER_USE[name] * ORDER[key]

        met = {}

        def meet(eng, name):
            met[name] = met.get(name, 0) + 1
            eng.drain().then_inc(S("stage_done"), 1)
            eng.wait_ge(S("stage_done"), 4 * met[name])

        def sp_constants(sp):
            for name, t in (("ident", ident), ("upper", upper), ("upstrict", upstrict), ("lowstrict", lowstrict)):
                sp.dma_start(t[:], A["k_" + name]).then_inc(S("constants"), 16)
            sp.dma_start(cT[:, 0], A["c"].rearrange("a (t p) -> p (a t)", p=P)).then_inc(S("constants"), 16)
            sp.dma_start(cT[:, 1], A["c_2"].rearrange("a (t p) -> p (a t)", p=P)).then_inc(S("constants"), 16)
            sp.dma_start(X[:], A["x"].rearrange("a (t p) d -> p (a t) d", p=P)).then_inc(S("constants"), 16)

        N_CONST = 7 * 16

        ada_bias = work[0:1, 0:6 * D]
        ada_bias2 = work[0:1, 6 * D:6 * D + 3 * D]
        ada_row = work[0:1, 10 * D:10 * D + 2 * CH].rearrange("p (b n) -> p b n", b=2)
        ada_acc = work[:, 11 * D:11 * D + 2 * CH].rearrange("p (b n) -> p b n", b=2)
        w2v = A["ada_w_2"].rearrange("l s k n -> (l s) k n")
        b2v = A["ada_b_2"].rearrange("l s n -> (l s) n")
        N_ADA = 36

        def ada_sp(sp):
            sp.dma_start(ada_bias, A["b_ada"]).then_inc(S("ada_bias_in"), 16)
            w = A["w_ada"][0]
            with sp.Fori(0, 2) as i:
                for s in range(6):
                    sp.wait_ge(freed[s], i + 1)
                    sp.dma_start(slots[:, s], wview(w[:, bass.ds(i * 6 * CH + s * CH, CH)])).then_inc(landed[s], 16)
            with sp.Fori(0, 4) as i:
                for s in range(6):
                    sp.wait_ge(freed[s], i + 3)
                    sp.dma_start(slots[:, s], wview(w2v[i, :, s * CH:(s + 1) * CH])).then_inc(landed[s], 16)
                sp.wait_ge(S("ada_bias2_used"), i + 1)
                sp.dma_start(ada_bias2, b2v[bass.ds(i, 1), :]).then_inc(S("ada_bias_in"), 16)
            for s in range(6):
                loads[s] = 6

        def ada_chunk_dve(v, i, s, which, n):
            acc = ada_acc[:, s % 2]
            v.wait_ge(landed[s], i * 16 + 16)
            v.wait_ge(S("ada_acc_free"), n + 1)
            v.tensor_scalar(acc, slots[:, s, 0], cT[:, which, 0:1], None, ALU.mult)
            for t in range(1, KT):
                v.drain()
                ins = v.scalar_tensor_tensor(acc, slots[:, s, t], cT[:, which, t:t + 1], acc, ALU.mult, ALU.add)
            ins.then_inc(freed[s], 1)
            v.drain()

        def ada_dve(v):
            v.wait_ge(S("c_silu"), 1)
            v.wait_ge(S("ada_bias_in"), 16)
            with v.Fori(0, 2) as i:
                for s in range(6):
                    ada_chunk_dve(v, i, s, 0, i * 6 + s)
                    acc = ada_acc[0:1, s % 2]
                    v.tensor_tensor(acc, acc, ada_bias[:, bass.ds(i * 6 * CH + s * CH, CH)],
                                    ALU.add).then_inc(S("ada_acc_ready"), 1)
            v.nop().then_inc(S("ada_bias2_used"), 1)
            with v.Fori(0, 4) as i:
                for s in range(6):
                    ada_chunk_dve(v, i + 2, s, 1, i * 6 + s + 12)
                    acc = ada_acc[0:1, s % 2]
                    if s == 0:
                        v.wait_ge(S("ada_bias_in"), i * 16 + 32)
                    v.tensor_tensor(acc, acc, ada_bias2[:, s * CH:(s + 1) * CH],
                                    ALU.add).then_inc(S("ada_acc_ready"), 1)
                v.drain().then_inc(S("ada_bias2_used"), 1)

        def ada_pe(pe):
            for s in range(6):
                pe.nop().then_inc(freed[s], 1)
            pe.nop().then_inc(S("ada_acc_free"), 2)
            pe.wait_ge(S("ones_ready"), 1)
            with pe.Fori(0, N_ADA // 2) as i:
                for b in range(2):
                    pe.wait_ge(S("ada_acc_ready"), i * 2 + b + 1)
                    pe.wait_ge(S("ada_row_free"), i * 2 + b + 1)
                    pe.matmul(ps[0:1, b], ones[:, 0:1], ada_acc[:, b], start=True, stop=True
                              ).then_inc(S("ada_acc_free"), 1)

        def ada_act(a):
            a.wait_ge(S("constants"), N_CONST)
            a.activation(cT[:], cT[:], ACT.Silu).then_inc(S("c_silu"), 1)
            a.nop().then_inc(S("ada_row_free"), 2)
            a.nop().then_inc(S("ada_out"), 16)
            with a.Fori(0, N_ADA // 2) as i:
                for b in range(2):
                    a.wait_ge(S("ada_acc_free"), i * 2 + b + 3)
                    a.wait_ge(S("ada_out"), i * 32 + b * 16 + 16)
                    a.copy(ada_row[:, b], ps[0:1, b]).then_inc(S("ada_row_free"), 1)
                    a.drain()
                    a.dma_start(mod_dram[:, bass.ds(i * 2 * CH + b * CH, CH)], ada_row[:, b]).then_inc(S("ada_out"), 16)
            a.wait_ge(S("ada_out"), N_ADA * 16 + 16)

        def ada_pool(g):
            g.memset(epsc[:, 0:1], EPS * DD)
            g.memset(epsc[:, 1:2], EPS)
            g.memset(ones[:], 1.0).then_inc(S("ones_ready"), 1)

        def mod_load(sp, key, scale_at, shift_at, gate_at, norm=None):
            for dst, at in ((modA, scale_at), (modB, shift_at), (modG, gate_at)):
                sp.dma_start(dst[:], mod_dram[0:1, at:at + D].broadcast_to([P, D])).then_inc(S("mod_in"), 16)
            if norm is not None:
                sp.dma_start(tmp[:], norm.broadcast_to([P, D])).then_inc(S("mod_in"), 16)

        def rms_scales_dve(v, key):
            for t in range(TT):
                v.tensor_tensor_reduce(stage[:], X[:, t], X[:, t], 1.0, 0.0, ALU.mult, ALU.add, small[:, t:t + 1])
                v.drain()
            v.tensor_scalar(small[:, 4:8], small[:, 0:4], 1.0 / D, EPS, ALU.mult, ALU.add).then_inc(S("var"), 1)
            v.wait_ge(S("sd"), before("sd", key) + 1)
            v.reciprocal(small[:, 0:4], small[:, 8:12])
            v.drain()

        def rms_scales_act(a, key):
            a.wait_ge(S("var"), before("var", key) + 1)
            a.activation(small[:, 8:12], small[:, 4:8], ACT.Sqrt).then_inc(S("sd"), 1)

        def norm_dve(v, key, rms, store=None):
            v.wait_ge(S("mod_in"), before("mod_in", key) + (64 if rms else 48))
            v.tensor_scalar(modA[:], modA[:], 1.0, None, ALU.add)
            v.drain()
            if rms:
                v.tensor_tensor(modA[:], modA[:], tmp[:], ALU.mult)
                rms_scales_dve(v, key)
            if rms:
                with v.Fori(0, TT) as t:
                    v.wait_ge(S("stage_free"), t + 1 + before("stage_free", key))
                    if store:
                        v.wait_ge(S("h2_tile"), t + 1)
                    v.scalar_tensor_tensor(stage[:], X[:, t], small[:, bass.ds(t, 1)], modA[:], ALU.mult, ALU.mult)
                    v.drain()
                    v.tensor_tensor(stage[:], stage[:], modB[:], ALU.add).then_inc(S("stage_ready"), 1)
            else:
                for t in range(TT):
                    dst = (stage, tmp)[t % 2]
                    if t >= 2:
                        v.wait_ge(S("stage_free"), t + before("stage_free", key))
                    v.tensor_tensor(dst[:], X[:, t], modA[:], ALU.mult)
                    v.drain()
                    v.tensor_tensor(dst[:], dst[:], modB[:], ALU.add).then_inc(S("stage_ready"), 1)

        def turn_pe(pe, key, staged=1):
            pe.nop().then_inc(S("stage_free"), 1)
            with pe.Fori(0, TT // staged) as i:
                for j in range(staged):
                    t = i * staged + j
                    src = (stage, tmp)[j]
                    pe.wait_ge(S("stage_ready"), t + 1 + before("stage_ready", key))
                    pe.wait_ge(S("turned_out"), t + 1 + before("turned_out", key))
                    for k in range(KT):
                        ins = pe.transpose(ps[:, 6 + k // 4, (k % 4) * P:(k % 4 + 1) * P], src[:, k * P:(k + 1) * P], ident[:])
                    ins.then_inc(S("stage_free"), 1)

        def turn_act(a, key):
            a.nop().then_inc(S("turned_out"), 1)
            with a.Fori(0, TT) as t:
                a.wait_ge(S("stage_free"), t + 2 + before("stage_free", key))
                a.copy(hT[:, :, bass.ds(t * P, P)],
                       ps[:, 6:8].rearrange("p b (k n) -> p (b k) n", n=P)).then_inc(S("turned_out"), 1)

        qkvT = work[:, 0:6144].rearrange("p (m t) -> p m t", m=12)
        swtok = work[:, 6144:9216].rearrange("p (t n) -> p t n", t=TT)
        mixed = work[:, 9216:13312].rearrange("p (t n) -> p t n", t=TT)
        wab = sb("wab", [P, KT, 2 * DH])
        convw = sb("convw", [P, 12, 4])
        W_IN = A["w_in"][0]

        def proj_sp(sp):
            sp.dma_start(wab[:], wview(W_IN[:, 2048:2056])).then_inc(S("wab_in"), 16)
            for w in range(4):
                sp.dma_start(convw[:, :, w], A["conv_w"][0, w:w + 1].rearrange("a (m p) -> p (a m)", p=P)).then_inc(S("conv_in"), 16)
            for s in range(4):
                load(sp, s, wview(W_IN[:, s * CH:(s + 1) * CH]))
            load(sp, 4, wview(W_IN[:, 2056:2568]))
            load(sp, 5, wview(W_IN[:, 2568:2824]), slots[:, 5, :, 0:256])

        def proj_pe(pe):
            groups = []
            for s in range(3):
                take(pe, s)
                for m in range(4):
                    pe.wait_ge(S("bank_free"), before("bank_free", "q") + s * 4 + m + 1)
                    for k in range(KT):
                        ins = pe.matmul(ps[:, m], slots[:, s, k, m * P:(m + 1) * P], hT[:, k, :], start=k == 0, stop=k == KT - 1)
                    ins.then_inc(S("product"), 1)
                pe.drain().then_inc(freed[s], 1)
            for s, cols in ((3, CH), (4, CH), (5, 256)):
                take(pe, s)
                for t in range(TT):
                    if s == 3:
                        pe.wait_ge(S("bank_free"), before("bank_free", "q") + 12 + t + 1)
                    else:
                        pe.wait_ge(S("z_read" if s == 4 else "sw_read"), t + 1)
                    for k in range(KT):
                        ins = pe.matmul(ps[:, t, 0:cols], hT[:, k, t * P:(t + 1) * P], slots[:, s, k, 0:cols], start=k == 0, stop=k == KT - 1)
                    ins.then_inc(S("product"), 1)
                pe.drain().then_inc(freed[s], 1)
            pe.wait_ge(S("wab_in"), 16)
            for n in range(NC):
                for k in range(KT):
                    ins = pe.matmul(ps[0:C, 4, n * 8:(n + 1) * 8], hT[:, k, n * C:(n + 1) * C], wab[:, k], start=k == 0, stop=k == KT - 1)
            ins.then_inc(S("product_ab"), 1)

        def proj_dve(v):
            v.wait_ge(S("conv_in"), 64)
            v.nop().then_inc(S("bank_free"), 4)
            for j in range(12):
                u, y = ps[:, j % 4], stage[:, (j % 2) * CH:(j % 2 + 1) * CH]
                v.wait_ge(S("product"), before("product", "q") + j + 1)
                if j >= 2:
                    v.wait_ge(S("conv_silu"), j - 1)
                v.tensor_scalar(y, u, convw[:, j, 3:4], None, ALU.mult)
                for w in (2, 1, 0):
                    v.drain()
                    ins = v.scalar_tensor_tensor(y[:, 3 - w:], u[:, 0:T - 3 + w], convw[:, j, w:w + 1], y[:, 3 - w:], ALU.mult, ALU.add)
                ins.then_inc(S("conv_ready"), 1)
                v.drain().then_inc(S("bank_free"), 1)
            for t in range(TT):
                v.wait_ge(S("product"), before("product", "q") + 16 + t + 1)
                v.tensor_copy(swtok[:, t, 0:CH], ps[:, t]).then_inc(S("sw_read"), 1)
            for t in range(TT):
                v.wait_ge(S("product"), before("product", "q") + 20 + t + 1)
                v.tensor_copy(swtok[:, t, CH:768], ps[:, t, 0:256])

        def proj_act(a):
            for j in range(12):
                a.wait_ge(S("conv_ready"), j + 1)
                a.activation(qkvT[:, j], stage[:, (j % 2) * CH:(j % 2 + 1) * CH], ACT.Silu).then_inc(S("conv_silu"), 1)
            for t in range(TT):
                a.wait_ge(S("product"), before("product", "q") + 12 + t + 1)
                a.activation(mixed[:, t, 0:CH], ps[:, t], ACT.Silu).then_inc(S("z_read"), 1)


        grow = scratch[:, 0:2048].rearrange("p (s c) -> p s c", c=C)
        dec = scratch[0:C, 2048:4096].rearrange("p (s c) -> p s c", c=C)
        akk = scratch[0:C, 4096:6144].rearrange("p (s c) -> p s c", c=C)
        aqkT = scratch[0:C, 6144:8192].rearrange("p (s c) -> p s c", c=C)
        tinvT = scratch[0:C, 8192:10240].rearrange("p (s c) -> p s c", c=C)
        asol = scratch[:, 10240:14336].rearrange("p (r s) -> p r s", r=C)
        xT = scratch[:, 14336:15360].rearrange("p (c r) -> p c r", r=C)
        prod = scratch[:, 15360:16384].rearrange("p (c r) -> p c r", r=C)
        gcol, beta, kdec_s, kb_s = (small[0:C, 128 + 32 * j:160 + 32 * j] for j in range(4))
        red = small[:, 16:32]
        consts16 = sb("consts16", [P, 16])
        g_s = sb("g_s", [P, 96])
        cdec = sb("cdec", [P, NS])
        a_dram = dram("a_dram", (NS, C, C))
        x_dram = dram("x_dram", (NS, 4, C // 4, C))

        def hn(ap):
            return ap.rearrange("p (h n) -> p n h", h=DH)

        def dn1_moves(sp):
            sp.dma_start(consts16[:, 0:4], A["a_log"].broadcast_to([P, 4])).then_inc(S("dn_in"), 16)
            sp.dma_start(consts16[:, 4:8], A["dt_bias"].broadcast_to([P, 4])).then_inc(S("dn_in"), 16)
            sp.wait_ge(S("akk_ready"), 1)
            sp.dma_start(a_dram.rearrange("s c r -> c s r"), akk).then_inc(S("akk_out"), 16)
            sp.wait_ge(S("akk_out"), 16)
            for q in range(4):
                sp.dma_start(asol[q * 32:(q + 1) * 32].rearrange("p r s -> p (r s)"),
                             a_dram.rearrange("s c r -> s (c r)")).then_inc(S("asol_in"), 16)
            sp.wait_ge(S("solved"), 1)
            for q in range(4):
                sp.dma_start(x_dram[:, q].rearrange("s c r -> s (c r)"),
                             xT[q * 32:(q + 1) * 32].rearrange("p c r -> p (c r)")).then_inc(S("x_out"), 16)
            sp.wait_ge(S("x_out"), 64)
            sp.dma_start(tinvT, x_dram.rearrange("s q c r -> (q c) s r")).then_inc(S("tinv_in"), 16)

        def dn1_pe(pe):
            for j in range(8):
                pe.wait_ge(S("sq_ready"), j + 1)
                if j >= 2:
                    pe.wait_ge(S("norm_used"), j - 1)
                pe.matmul(ps[:, j % 2], ones[:], stage[:, (j % 2) * CH:(j % 2 + 1) * CH], start=True, stop=True).then_inc(S("sq_sum"), 1)
            pe.wait_ge(S("g_ready"), 1)
            pe.matmul(ps[0:C, 4, 0:NS], upper[0:C, 0:C], g_s[0:C, 0:NS], start=True, stop=True).then_inc(S("gcum_product"), 1)
            pe.wait_ge(S("gmask_ready"), 1)
            for j in range(4):
                ins = pe.matmul(ps[:, j], ones[0:C, :], tinvT[:, j * 8:(j + 1) * 8].rearrange("p s c -> p (s c)"), start=True, stop=True)
            ins.then_inc(S("gcum_product"), 1)
            pe.wait_ge(S("unit_done"), 8)
            pe.wait_ge(S("grow_out"), 1)
            pe.wait_ge(S("gcol_out"), 1)
            for h in range(DH):
                for n in range(NC):
                    kc = qkvT[:, 4 + h, n * C:(n + 1) * C]
                    pe.matmul(ps[0:C, h, n * C:(n + 1) * C], kc, kc, start=True, stop=True)
                    ins = pe.matmul(ps[0:C, 4 + h, n * C:(n + 1) * C], kc, qkvT[:, h, n * C:(n + 1) * C], start=True, stop=True)
            ins.then_inc(S("kk_ps"), 1)

        def dn1_act(a):
            for j in range(8):
                if j >= 2:
                    a.wait_ge(S("sq_sum"), j - 1)
                a.activation(stage[:, (j % 2) * CH:(j % 2 + 1) * CH], qkvT[:, j], ACT.Square).then_inc(S("sq_ready"), 1)
                if j >= 1:
                    dn1_act_norm(a, j - 1)
            dn1_act_norm(a, 7)
            a.wait_ge(S("ab_ready"), 1)
            a.activation(g_s[0:C, 32:64], gab_abs, ACT.Exp, scale=-1.0)
            a.activation(consts16[:, 8:12], consts16[:, 0:4], ACT.Exp)
            a.drain()
            a.activation(g_s[0:C, 32:64], g_s[0:C, 32:64], ACT.Ln, bias=1.0).then_inc(S("sp_ln"), 1)
            a.activation(beta, g_s[0:C, 64:96], ACT.Sigmoid).then_inc(S("beta_ready"), 1)
            a.wait_ge(S("gcum_product"), 2)
            a.copy(grow.rearrange("p (b s) c -> p b (s c)", b=4), ps[:, 0:4]).then_inc(S("grow_out"), 1)
            a.wait_ge(S("dec_diff"), 1)
            a.activation(dec, dec, ACT.Exp).then_inc(S("dec_exp"), 1)
            a.wait_ge(S("dec_diff"), 2)
            a.activation(dec, dec, ACT.Exp).then_inc(S("dec_exp"), 1)
            a.activation(kdec_s, kdec_s, ACT.Exp)
            a.activation(cdec[:], grow[:, :, C - 1], ACT.Exp)
            a.activation(kb_s, gcol, ACT.Exp)
            a.wait_ge(S("grow_used"), 1)
            a.drain()
            a.activation(grow, grow, ACT.Exp).then_inc(S("exps"), 1)

        gab_abs = g_s[0:C, 32:64]

        def dn1_act_norm(a, j):
            a.wait_ge(S("sq_sum"), j + 1)
            if j >= 2:
                a.wait_ge(S("unit_done"), j - 1)
            f = float(DD) if j < 4 else 1.0
            a.activation(tmp[:, (j % 2) * CH:(j % 2 + 1) * CH], ps[:, j % 2], ACT.Sqrt, scale=f, bias=epsc[:, 0:1] if j < 4 else epsc[:, 1:2]).then_inc(S("norm_used"), 1)

        def dn1_dve(v):
            for j in range(8):
                t = tmp[:, (j % 2) * CH:(j % 2 + 1) * CH]
                v.wait_ge(S("norm_used"), j + 1)
                v.reciprocal(t, t)
                v.drain()
                v.tensor_tensor(qkvT[:, j], qkvT[:, j], t, ALU.mult).then_inc(S("unit_done"), 1)
            v.wait_ge(S("product_ab"), 1)
            v.wait_ge(S("dn_in"), 32)
            ab = ps[0:C, 4, 0:64].rearrange("p (n j) -> p n j", j=8)
            v.tensor_copy(hn(g_s[0:C, 64:96]), ab[:, :, 4:8])
            v.tensor_tensor(hn(g_s[0:C, 0:32]), ab[:, :, 0:4], consts16[0:C, 4:8].unsqueeze(1).broadcast_to([C, NC, 4]), ALU.add)
            v.drain()
            v.tensor_scalar(g_s[0:C, 32:64], g_s[0:C, 0:32], -1.0, None, ALU.mult)
            v.drain()
            v.tensor_tensor(g_s[0:C, 32:64], g_s[0:C, 32:64], g_s[0:C, 0:32], ALU.max).then_inc(S("ab_ready"), 1)
            v.wait_ge(S("sp_ln"), 1)
            v.scalar_tensor_tensor(g_s[0:C, 0:32], g_s[0:C, 0:32], 0.0, g_s[0:C, 32:64], ALU.max, ALU.add)
            v.tensor_scalar(consts16[:, 8:12], consts16[:, 8:12], -1.0, None, ALU.mult)
            v.drain()
            v.tensor_tensor(hn(g_s[0:C, 0:32]), hn(g_s[0:C, 0:32]), consts16[0:C, 8:12].unsqueeze(1).broadcast_to([C, NC, 4]), ALU.mult).then_inc(S("g_ready"), 1)
            v.drain()
            gm = tinvT
            v.tensor_tensor(gm, g_s[0:C, 0:32].unsqueeze(2).broadcast_to([C, NS, C]),
                            upper[0:C, 0:C].unsqueeze(1).broadcast_to([C, NS, C]), ALU.mult).then_inc(S("gmask_ready"), 1)
            v.wait_ge(S("gcum_product"), 1)
            v.tensor_copy(gcol, ps[0:C, 4, 0:NS]).then_inc(S("gcol_out"), 1)
            v.drain()
            v.wait_ge(S("grow_out"), 1)
            v.tensor_tensor(kdec_s, grow[0:C, :, C - 1], gcol, ALU.subtract)
            gc = gcol.unsqueeze(2).broadcast_to([C, NS, C])
            v.tensor_tensor(dec, gc, grow[0:C], ALU.subtract)
            v.drain()
            v.tensor_scalar(dec, dec, 0.0, None, ALU.min).then_inc(S("dec_diff"), 1)
            v.wait_ge(S("dec_exp"), 1)
            v.tensor_tensor(dec, dec, lowstrict[0:C, 0:C].unsqueeze(1).broadcast_to([C, NS, C]), ALU.mult)
            v.wait_ge(S("beta_ready"), 1)
            v.wait_ge(S("kk_ps"), 1)
            v.drain()
            v.tensor_tensor(dec, dec, beta.unsqueeze(2).broadcast_to([C, NS, C]), ALU.mult)
            v.drain()
            v.tensor_tensor(akk.rearrange("p (b s) c -> p b (s c)", b=4), dec.rearrange("p (b s) c -> p b (s c)", b=4), ps[0:C, 0:4], ALU.mult).then_inc(S("akk_ready"), 1)
            v.drain()
            v.tensor_tensor(dec, grow[0:C], gc, ALU.subtract).then_inc(S("grow_used"), 1)
            v.drain()
            v.tensor_scalar(dec, dec, 0.0, None, ALU.min).then_inc(S("dec_diff"), 1)
            v.wait_ge(S("dec_exp"), 2)
            v.tensor_tensor(dec, dec, upper[0:C, 0:C].unsqueeze(1).broadcast_to([C, NS, C]), ALU.mult)
            v.drain()
            v.tensor_tensor(aqkT.rearrange("p (b s) c -> p b (s c)", b=4), dec.rearrange("p (b s) c -> p b (s c)", b=4), ps[0:C, 4:8], ALU.mult)
            v.wait_ge(S("exps"), 1)
            for h in range(DH):
                v.tensor_tensor(qkvT[:, h], qkvT[:, h], grow[:, h * NC:(h + 1) * NC].rearrange("p s c -> p (s c)"), ALU.mult)
            v.drain()
            v.wait_ge(S("xT_init"), 1)
            v.wait_ge(S("asol_in"), 64)
            for part in range(4):
                n = 16 * (part + 1)
                with v.Fori(16 * part, n) as r:
                    row = asol[:, bass.ds(r, 1), 0:n].broadcast_to([P, 16, n])
                    v.tensor_tensor(prod[:, :, 0:n], xT[:, :, 0:n], row, ALU.mult)
                    v.drain()
                    v.tensor_reduce(red, prod[:, :, 0:n], AX_X, ALU.add)
                    v.drain()
                    col = xT[:, :, bass.ds(r, 1)]
                    v.tensor_tensor(col, col, red.unsqueeze(2), ALU.subtract)
                    v.drain()
            v.drain().then_inc(S("solved"), 1)

        def dn1_pool(g):
            g.memset(xT, 0.0)
            g.drain()
            for q in range(4):
                for c in range(16):
                    ins = g.memset(xT[q * 32:(q + 1) * 32, c, q * 16 + c:q * 16 + c + 1], 1.0)
            ins.then_inc(S("xT_init"), 1)

        B0 = 10240
        ktok, vtok, kbt, vbt, kdt, vnew, usb = (
            scratch[0:C, B0 + j * 512:B0 + (j + 1) * 512].rearrange("p (h d) -> p h d", h=DH) for j in range(7))
        wT = scratch[:, B0 + 3584:B0 + 3840].rearrange("p (h c) -> p h c", h=DH)
        st = scratch[:, B0 + 4096:B0 + 4608].rearrange("p (h d) -> p h d", h=DH)
        o_ss = small[:, 32:48]

        def sysn(t, n):
            return t.rearrange("p (h n) -> p h n", h=DH)[:, :, n]

        def dn2_pe(pe):
            pe.wait_ge(S("tinv_in"), 16)
            for n in range(NC):
                tok = slice(n * C, (n + 1) * C)
                if n:
                    pe.wait_ge(S("kb_ready"), n)
                for h in range(DH):
                    pe.transpose(ps[0:C, 0, h * DD:(h + 1) * DD], qkvT[:, 4 + h, tok], ident[:])
                    ins = pe.transpose(ps[0:C, 1, h * DD:(h + 1) * DD], qkvT[:, 8 + h, tok], ident[:])
                ins.then_inc(S("tok_ps"), 1)
                pe.wait_ge(S("kb_ready"), n + 1)
                if n:
                    pe.wait_ge(S("v_new"), n)
                for h in range(DH):
                    ti = tinvT[:, h * NC + n]
                    pe.matmul(ps[:, 2, h * C:(h + 1) * C], kbt[:, h], ti, start=True, stop=True)
                    ins = pe.matmul(ps[0:C, 3, h * DD:(h + 1) * DD], ti, vbt[:, h], start=True, stop=True)
                ins.then_inc(S("uw_ps"), 1)
                pe.wait_ge(S("wT_out"), n + 1)
                pe.wait_ge(S("state"), n + 1)
                for h in range(DH):
                    ins = pe.matmul(ps[0:C, 4, h * DD:(h + 1) * DD], wT[:, h], st[:, h], start=True, stop=True)
                ins.then_inc(S("ws_ps"), 1)
                if n:
                    pe.wait_ge(S("o_out"), n)
                pe.wait_ge(S("v_new"), n + 1)
                for h in range(DH):
                    pe.matmul(ps[0:C, 5, h * DD:(h + 1) * DD], qkvT[:, h, tok], st[:, h], start=True, stop=False)
                    pe.matmul(ps[0:C, 5, h * DD:(h + 1) * DD], aqkT[:, h * NC + n], vnew[:, h], start=False, stop=True)
                for h in range(DH):
                    ins = pe.matmul(ps[:, 6, h * DD:(h + 1) * DD], kdt[:, h], vnew[:, h], start=True, stop=True)
                ins.then_inc(S("o_ps"), 1)

        def dn2_dve(v):
            v.memset(st, 0.0).then_inc(S("state"), 1)
            v.tensor_tensor(kb_s, kb_s, beta, ALU.mult)
            v.drain()
            for n in range(NC):
                v.wait_ge(S("tok_ps"), n + 1)
                kp = ps[0:C, 0].rearrange("p (h d) -> p h d", h=DH)
                vp = ps[0:C, 1].rearrange("p (h d) -> p h d", h=DH)

                def per(s):
                    return sysn(s, n).unsqueeze(2).broadcast_to([C, DH, DD])
                v.tensor_tensor(kdt, kp, per(kdec_s), ALU.mult)
                v.tensor_tensor(kbt, kp, per(kb_s), ALU.mult)
                v.tensor_tensor(vbt, vp, per(beta), ALU.mult).then_inc(S("kb_ready"), 1)
                v.wait_ge(S("uw_ps"), n + 1)
                v.tensor_copy(wT, ps[:, 2, 0:DH * C].rearrange("p (h c) -> p h c", h=DH)).then_inc(S("wT_out"), 1)
                v.tensor_copy(usb, ps[0:C, 3].rearrange("p (h d) -> p h d", h=DH))
                v.wait_ge(S("ws_ps"), n + 1)
                v.drain()
                v.tensor_tensor(vnew, usb, ps[0:C, 4].rearrange("p (h d) -> p h d", h=DH), ALU.subtract).then_inc(S("v_new"), 1)
                v.wait_ge(S("o_ps"), n + 1)
                v.tensor_tensor(st, st, sysn(cdec[:], n).unsqueeze(2).broadcast_to([P, DH, DD]), ALU.mult)
                v.drain()
                v.tensor_tensor(st, st, ps[:, 6].rearrange("p (h d) -> p h d", h=DH), ALU.add).then_inc(S("state"), 1)
                v.drain()

        otok = hT[:].rearrange("p k t -> p (k t)")[:, 0:2048].rearrange("p (t n) -> p t n", t=TT)

        def dn2_act(a):
            for n in range(NC):
                a.wait_ge(S("o_ps"), n + 1)
                a.copy(otok[(n % 2) * C:(n % 2 + 1) * C, n // 2], ps[0:C, 5]).then_inc(S("o_out"), 1)

        def mixer_loads(sp):
            sp.dma_start(dnw[:], A["dn_norm_w"].broadcast_to([P, DD])).then_inc(S("dnw_in"), 16)
            sp.dma_start(qnw[:, 0:SD], A["q_norm_w"].broadcast_to([P, SD])).then_inc(S("dnw_in"), 16)
            sp.dma_start(qnw[:, SD:2 * SD], A["k_norm_w"].broadcast_to([P, SD])).then_inc(S("dnw_in"), 16)
            sp.dma_start(sinks[:, 0:SH], A["sinks"].broadcast_to([P, SH])).then_inc(S("dnw_in"), 16)
            sp.dma_start(sinks[:, SH:2 * SH], A["attn_sinks_2"].broadcast_to([P, SH])).then_inc(S("dnw_in"), 16)

        dnw = sb("dnw", [P, DD])
        qnw = sb("qnw", [P, 2 * SD])
        sinks = sb("sinks", [P, 2 * SH])

        def dn3_dve(v):
            v.wait_ge(S("dnw_in"), 80)
            for t in range(TT):
                v.tensor_tensor(stage[:, 0:CH], otok[:, t], otok[:, t], ALU.mult)
                v.drain()
                v.tensor_reduce(o_ss[:, t * DH:(t + 1) * DH], stage[:, 0:CH].rearrange("p (h d) -> p h d", h=DH), AX_X, ALU.add)
                v.drain()
            v.tensor_scalar(o_ss, o_ss, 1.0 / DD, EPS, ALU.mult, ALU.add).then_inc(S("var"), 1)
            v.wait_ge(S("sd"), before("sd", "dn") + 1)
            v.reciprocal(o_ss, o_ss)
            v.drain()
            for t in range(TT):
                o = otok[:, t].rearrange("p (h d) -> p h d", h=DH)
                m = mixed[:, t, 0:CH].rearrange("p (h d) -> p h d", h=DH)
                v.tensor_tensor(o, o, o_ss[:, t * DH:(t + 1) * DH].unsqueeze(2).broadcast_to([P, DH, DD]), ALU.mult)
                v.tensor_tensor(m, m, dnw[:].unsqueeze(1).broadcast_to([P, DH, DD]), ALU.mult)
                v.drain()
                v.tensor_tensor(m, m, o, ALU.mult)

        def dn3_act(a):
            a.wait_ge(S("var"), before("var", "dn") + 1)
            a.activation(o_ss, o_ss, ACT.Sqrt).then_inc(S("sd"), 1)

        swb = scratch[:, 0:2048].rearrange("p (h n) -> p h n", h=SH)
        lg = scratch[:, 2048:4096].rearrange("p (h n) -> p h n", h=SH)
        pT = scratch[:, 4096:6144].rearrange("p (j n) -> p j n", j=16)
        sqn = scratch[:, 6144:6784]
        qTc = scratch[:, 6912:7424].rearrange("p (j n) -> p j n", j=4)
        kTw = scratch[:, 7424:7680]
        vw = scratch[:, 7680:7936].rearrange("p (b n) -> p b n", b=2)
        sq = scratch[:, 7936:8576]
        NH = SH + SG

        def sw_load(sp):
            sp.dma_start(swb, A["k_swbias"].rearrange("p (h n) -> p h n", h=SH)).then_inc(S("swb_in"), 16)

        def sw_dve(v):
            v.memset(kTw, 0.0)
            v.memset(vw, 0.0)
            v.wait_ge(S("swb_in"), 16)
            v.drain()
            with v.Fori(0, TT) as t:
                row = swtok[:, t, 0:640]
                v.tensor_tensor(sq, row, row, ALU.mult)
                v.drain()
                v.tensor_reduce(small[:, 0:NH], sq.rearrange("p (h d) -> p h d", d=SD), AX_X, ALU.add)
                v.drain()
                v.tensor_scalar(small[:, 0:NH], small[:, 0:NH], 1.0 / SD, EPS, ALU.mult, ALU.add).then_inc(S("sw_ms"), 1)
                v.wait_ge(S("sw_rms"), t + 1)
                v.reciprocal(small[:, 0:NH], small[:, 0:NH])
                v.drain()
                qn = sqn[:, 0:512].rearrange("p (j g d) -> p g j d", j=SQ, g=SG)
                v.tensor_tensor(qn, swtok[:, t, 0:512].rearrange("p (g j d) -> p g j d", g=SG, j=SQ),
                                small[:, 0:SH].rearrange("p (g j) -> p g j", g=SG).unsqueeze(3).broadcast_to([P, SG, SQ, SD]), ALU.mult)
                kn = sqn[:, 512:640].rearrange("p (g d) -> p g d", g=SG)
                v.tensor_tensor(kn, swtok[:, t, 512:640].rearrange("p (g d) -> p g d", g=SG),
                                small[:, SH:NH].unsqueeze(2).broadcast_to([P, SG, SD]), ALU.mult)
                v.drain()
                q8 = sqn[:, 0:512].rearrange("p (h d) -> p h d", d=SD)
                v.tensor_tensor(q8, q8, qnw[:, 0:SD].unsqueeze(1).broadcast_to([P, SH, SD]), ALU.mult)
                v.tensor_tensor(kn, kn, qnw[:, SD:2 * SD].unsqueeze(1).broadcast_to([P, SG, SD]), ALU.mult)
                v.tensor_copy(kTw[:, 0:P], kTw[:, P:2 * P])
                v.tensor_copy(vw[:, 0], vw[:, 1])
                v.drain()
                v.tensor_copy(vw[:, 1], swtok[:, t, 640:768]).then_inc(S("att_normed"), 1)
                v.wait_ge(S("att_turned"), t + 1)
                v.tensor_copy(qTc, ps[:, 4].rearrange("p (j n) -> p j n", j=4))
                v.tensor_copy(kTw[:, P:2 * P], ps[:, 5, 0:P]).then_inc(S("att_qk_ready"), 1)
                v.wait_ge(S("att_scores"), t + 1)
                v.scalar_tensor_tensor(lg.rearrange("p h n -> p (h n)"), ps[:, 0:4].rearrange("p b n -> p (b n)"), SD ** -0.5, swb.rearrange("p h n -> p (h n)"), ALU.mult, ALU.add)
                v.drain()
                v.tensor_scalar(lg[:, :, 0:P], lg[:, :, 0:P], edge[:, bass.ds(t, 1)], None, ALU.add)
                v.drain()
                v.tensor_reduce(small[:, 16:24], lg, AX_X, ALU.max)
                v.drain()
                v.tensor_tensor(small[:, 16:24], small[:, 16:24], sinks[:, 0:SH], ALU.max)
                v.drain()
                v.tensor_tensor(small[:, 24:32], sinks[:, 0:SH], small[:, 16:24], ALU.subtract)
                v.tensor_scalar(small[:, 40:48], small[:, 16:24], -1.0, None, ALU.mult)
                v.drain().then_inc(S("att_shifted"), 1)
                v.wait_ge(S("att_exp"), t + 1)
                v.tensor_tensor(small[:, 32:40], small[:, 32:40], small[:, 24:32], ALU.add)
                v.drain()
                v.reciprocal(small[:, 32:40], small[:, 32:40])
                v.drain()
                v.wait_ge(S("att_pv"), t + 1)
                v.tensor_tensor(mixed[:, t, CH:2 * CH].rearrange("p (h d) -> p h d", h=SH), ps[:, 4].rearrange("p (h d) -> p h d", h=SH),
                                small[:, 32:40].unsqueeze(2).broadcast_to([P, SH, SD]), ALU.mult).then_inc(S("att_tile_done"), 1)

        edge = sb("edge", [P, TT])

        def sw_act(a):
            with a.Fori(0, TT) as t:
                a.wait_ge(S("sw_ms"), t + 1)
                a.activation(small[:, 0:NH], small[:, 0:NH], ACT.Sqrt).then_inc(S("sw_rms"), 1)
                a.wait_ge(S("att_shifted"), t + 1)
                for h in range(SH):
                    a.activation(lg[:, h], lg[:, h], ACT.Exp, bias=small[:, 40 + h:41 + h], accum_out=small[:, 32 + h:33 + h])
                a.activation(small[:, 24:32], small[:, 24:32], ACT.Exp).then_inc(S("att_exp"), 1)
                a.wait_ge(S("att_pturned"), t + 1)
                a.copy(pT.rearrange("p (b j) n -> p b (j n)", b=4), ps[:, 0:4]).then_inc(S("att_pT"), 1)

        def sw_pe(pe):
            pe.nop().then_inc(S("att_tile_done"), 1)
            with pe.Fori(0, TT) as t:
                pe.wait_ge(S("att_normed"), t + 1)
                for j in range(4):
                    pe.transpose(ps[:, 4, j * P:(j + 1) * P], sqn[:, j * P:(j + 1) * P], ident[:])
                pe.transpose(ps[:, 5, 0:P], sqn[:, 512:640], ident[:]).then_inc(S("att_turned"), 1)
                pe.wait_ge(S("att_qk_ready"), t + 1)
                for h in range(SH):
                    g, j = h // SQ, h % SQ
                    ins = pe.matmul(ps[:, h // 2, (h % 2) * 256:(h % 2 + 1) * 256], qTc[g * SD:(g + 1) * SD, j], kTw[g * SD:(g + 1) * SD], start=True, stop=True)
                ins.then_inc(S("att_scores"), 1)
                pe.wait_ge(S("att_exp"), t + 1)
                for j in range(16):
                    h, b = j // 2, j % 2
                    ins = pe.transpose(ps[:, j // 4, (j % 4) * P:(j % 4 + 1) * P], lg[:, h, b * P:(b + 1) * P], ident[:])
                ins.then_inc(S("att_pturned"), 1)
                pe.wait_ge(S("att_pT"), t + 1)
                for h in range(SH):
                    g = h // SQ
                    for b in range(2):
                        ins = pe.matmul(ps[:, 4, h * SD:(h + 1) * SD], pT[:, 2 * h + b], vw[:, b, g * SD:(g + 1) * SD], start=b == 0, stop=b == 1)
                ins.then_inc(S("att_pv"), 1)
                pe.wait_ge(S("att_tile_done"), t + 2)

        def sw_pool(g):
            sw_load(g)
            g.memset(edge[:, 0:1], NEG)
            g.memset(edge[:, 1:TT], 0.0)

        def turn_tiles_dve(v, key, src):
            with v.Fori(0, TT) as t:
                v.wait_ge(S("stage_free"), t + 1 + before("stage_free", key))
                v.tensor_copy(stage[:], src[:, t]).then_inc(S("stage_ready"), 1)

        def pair_sp(sp, w, s0):
            for h in range(2):
                load(sp, s0 + h, wview(w[:, h * CH:(h + 1) * CH]))

        def pair_pe(pe, key, s0):
            for h in range(2):
                take(pe, s0 + h)
                for t in range(TT):
                    pe.wait_ge(S("bank_free"), before("bank_free", key) + h * TT + t + 1)
                    for k in range(KT):
                        ins = pe.matmul(ps[:, t], hT[:, k, t * P:(t + 1) * P], slots[:, s0 + h, k], start=k == 0, stop=k == KT - 1)
                    ins.then_inc(S("product"), 1)
                pe.drain().then_inc(freed[s0 + h], 1)

        def pair_dve_residual(v, key):
            v.nop().then_inc(S("bank_free"), TT)
            for h in range(2):
                for t in range(TT):
                    v.wait_ge(S("product"), before("product", key) + h * TT + t + 1)
                    c = slice(h * CH, (h + 1) * CH)
                    v.tensor_tensor(stage[:, 0:CH], ps[:, t], modG[:, c], ALU.mult).then_inc(S("bank_free"), 1)
                    v.drain()
                    v.tensor_tensor(X[:, t, c], X[:, t, c], stage[:, 0:CH], ALU.add)
                    v.drain()

        wr = work[:, 13056:13312].rearrange("p (k e) -> p k e", k=KT)
        R0 = work[:, 0:2048]
        lgt = R0[:, 0:128].rearrange("p (t e) -> p t e", t=TT)
        brt = R0[:, 128:160]
        io32 = R0[:, 160:192]
        top = R0[:, 192:224].rearrange("p (t j) -> p t j", t=TT)
        topi = R0[:, 224:256].bitcast(U32).rearrange("p (t j) -> p t j", t=TT)
        oneh = R0[:, 256:768].rearrange("p (j e) -> p j e", e=E)
        mask = R0[:, 768:896].rearrange("p (t e) -> p t e", t=TT)
        place = R0[:, 896:1024].rearrange("p (t e) -> p t e", t=TT)
        ohp = R0[:, 1024:1536].rearrange("p (j e) -> p j e", e=E)
        idxf = R0[:, 1536:1552]
        slotf = R0[:, 1552:1568]
        sloti = R0[:, 1568:1584].bitcast(I32)
        ov = R0[:, 1600:1700]
        pairs = sb("pairs", [P, 32], I32)
        fill = R0[:, 1700:1990].bitcast(I32)
        gates = sb("gates", [P, 16])
        tab = sb("tab", [P, 2 * MAXB + 2], I32)
        tabf = sb("tabf", [P, 2 * MAXB + 2])
        ohE = sb("ohE", [96, MAXB])
        pmod = sb("pmod", [P, 1])
        list_dram = dram("list_dram", (LROWS, 2), I32)
        h2_dram = dram("h2_dram", (T, D))
        y_dram = dram("y_dram", (T * TOPK, D))
        bparts = work[0:96, 9728:11264].bitcast(BF16)
        braw = work[0:32, 2048:2048 + 3 * D]
        bres = work[0:32, 2048 + 3 * D:2048 + 6 * D]

        def route_loads(sp):
            sp.dma_start(wr, wview(A["w_router"][0])).then_inc(S("route_in"), 16)
            sp.dma_start(pmod[:], A["k_pmod"]).then_inc(S("route_in"), 16)
            sp.dma_start(pairs[:], A["k_pairs"]).then_inc(S("route_in"), 16)
            sp.dma_start(brt, A["b_router"].broadcast_to([P, E])).then_inc(S("route_in"), 16)
            sp.dma_start(io32, A["k_iota32"]).then_inc(S("route_in"), 16)
            sp.dma_start(braw[:, 0:2 * D], A["b_up"][0]).then_inc(S("route_in"), 16)
            sp.dma_start(braw[:, 2 * D:3 * D], A["b_down"][0]).then_inc(S("route_in"), 16)
            sp.dma_start(list_dram.rearrange("(p j) two -> p (j two)", p=P), fill).then_inc(S("list_filled"), 16)

        def route_fill(g):
            f = fill.rearrange("p (j two) -> p j two", two=2)
            g.memset(f[:, :, 0:1], 0)
            g.memset(f[:, :, 1:2], DUMMY)
            g.drain()

        def route_pool(g):
            g.wait_ge(S("list_filled"), 16)
            g.wait_ge(S("route_step"), 4)
            for j in range(TT * TOPK):
                g.indirect_dma_start(list_dram, bass.IndirectOffsetOnAxis(ap=sloti[:, j:j + 1], axis=0),
                                     pairs[:, 2 * j:2 * j + 2], None).then_inc(S("list_out"), 16)
            g.wait_ge(S("list_out"), 16 * TT * TOPK)

        def route_pe(pe):
            pe.wait_ge(S("route_in"), 7 * 16)
            for t in range(TT):
                for k in range(KT):
                    ins = pe.matmul(ps[:, 0, t * E:(t + 1) * E], hT[:, k, t * P:(t + 1) * P], wr[:, k], start=k == 0, stop=k == KT - 1)
            ins.then_inc(S("route_product"), 1)
            pe.wait_ge(S("route_step"), 2)
            for t in range(TT):
                for u in range(t + 1):
                    pe.matmul(ps[:, 1, t * E:(t + 1) * E], upstrict[:] if u == t else ones[:], mask[:, u], start=u == 0, stop=u == t)
            for u in range(TT):
                ins = pe.matmul(ps[0:E, 2, 0:1], mask[:, u], ones[:, 0:1], start=u == 0, stop=u == TT - 1)
            ins.then_inc(S("route_product"), 1)
            pe.wait_ge(S("route_step"), 3)
            pe.matmul(ps[0:E, 3, 0:1], upper[0:E, 0:E], ov[0:E, 1:2], start=True, stop=True).then_inc(S("route_product"), 1)
            pe.wait_ge(S("route_step"), 5)
            pe.matmul(ps[:, 4, 0:16], ones[0:E, :], ov[0:E, 16:32], start=True, stop=True)
            pe.matmul(ps[0:1, 5, 0:16], ov[0:E, 1:2], ov[0:E, 16:32], start=True, stop=True)
            pe.matmul(ps[0:1, 5, 16:17], ov[0:E, 1:2], ones[0:E, 0:1], start=True, stop=True).then_inc(S("route_product"), 1)

        def route_act(a):
            a.wait_ge(S("route_step"), 1)
            for t in range(TT):
                a.activation(gates[:, t * 4:t * 4 + 4], top[:, t, 0:4], ACT.Exp, bias=small[:, t:t + 1], accum_out=small[:, 8 + t:9 + t])
            a.drain().then_inc(S("gate_exp"), 1)

        def route_dve(v):
            v.wait_ge(S("route_in"), 7 * 16)
            v.wait_ge(S("route_product"), 1)
            v.tensor_tensor(lgt, ps[:, 0, 0:TT * E].rearrange("p (t e) -> p t e", t=TT), brt.unsqueeze(1).broadcast_to([P, TT, E]), ALU.add)
            v.drain()
            for t in range(TT):
                v.max(top[:, t], lgt[:, t])
            v.drain()
            for t in range(TT):
                v.max_index(topi[:, t], top[:, t], lgt[:, t])
            v.tensor_scalar(small[:, 0:4], top[:, :, 0], -1.0, None, ALU.mult).then_inc(S("route_step"), 1)
            v.drain()
            v.tensor_copy(idxf.rearrange("p (t j) -> p t j", t=TT), topi[:, :, 0:4])
            v.drain()
            v.tensor_tensor(oneh, io32.unsqueeze(1).broadcast_to([P, 16, E]), idxf.unsqueeze(2).broadcast_to([P, 16, E]), ALU.is_equal)
            v.drain()
            v.tensor_reduce(mask, oneh.rearrange("p (t j) e -> p t e j", t=TT), AX_X, ALU.add).then_inc(S("route_step"), 1)
            v.wait_ge(S("gate_exp"), 1)
            v.reciprocal(small[:, 8:12], small[:, 8:12])
            v.drain()
            g4 = gates[:].rearrange("p (t j) -> p t j", t=TT)
            v.tensor_tensor(g4, g4, small[:, 8:12].unsqueeze(2).broadcast_to([P, TT, 4]), ALU.mult)
            v.wait_ge(S("route_product"), 2)
            v.scalar_tensor_tensor(place, io32.unsqueeze(1).broadcast_to([P, TT, E]), float(T), ps[:, 1, 0:TT * E].rearrange("p (t e) -> p t e", t=TT), ALU.mult, ALU.add)
            v.tensor_copy(ov[0:E, 0:1], ps[0:E, 2, 0:1])
            v.drain()
            for t in range(TT):
                v.tensor_tensor(ohp[:, t * 4:t * 4 + 4], oneh[:, t * 4:t * 4 + 4], place[:, t:t + 1].broadcast_to([P, 4, E]), ALU.mult)
            v.tensor_scalar(ov[0:E, 2:3], ov[0:E, 0:1], float(BLK), None, ALU.is_gt)
            v.tensor_scalar(ov[0:E, 3:4], ov[0:E, 0:1], float(2 * BLK), None, ALU.is_gt)
            v.tensor_scalar(ov[0:E, 4:5], ov[0:E, 0:1], float(3 * BLK), None, ALU.is_gt)
            v.drain()
            v.tensor_reduce(slotf, ohp, AX_X, ALU.add)
            v.tensor_reduce(ov[0:E, 1:2], ov[0:E, 2:5], AX_X, ALU.add).then_inc(S("route_step"), 1)
            v.drain()
            v.tensor_copy(sloti, slotf).then_inc(S("route_step"), 1)
            v.wait_ge(S("route_product"), 3)
            v.tensor_copy(ov[0:E, 5:6], ps[0:E, 3, 0:1])
            v.drain()
            v.tensor_scalar(ov[0:E, 16:32], io32[0:E, 0:16], ov[0:E, 5:6], None, ALU.is_ge).then_inc(S("route_step"), 1)
            v.tensor_copy(tabf[0:1, 0:E], io32[0:1])
            v.tensor_scalar(tabf[0:1, MAXB:MAXB + E], io32[0:1], float(T), None, ALU.mult)
            v.tensor_scalar(ohE[:, 0:E], io32[0:96], pmod[0:96], None, ALU.is_equal)
            v.wait_ge(S("route_product"), 4)
            v.tensor_scalar(tabf[0:1, E:MAXB], ps[0:1, 4, 0:16], float(E - 1), None, ALU.min)
            v.tensor_copy(ov[:, 32:48], ps[:, 4, 0:16])
            v.tensor_copy(ov[0:1, 48:65], ps[0:1, 5, 0:17])
            v.drain()
            v.tensor_tensor(ov[0:1, 66:82], io32[0:1, 0:16], ov[0:1, 48:64], ALU.subtract)
            v.tensor_scalar(ohE[:, E:MAXB], ov[0:96, 32:48], pmod[0:96], None, ALU.is_equal)
            v.tensor_scalar(tabf[0:1, 2 * MAXB:2 * MAXB + 1], ov[0:1, 64:65], float(E), None, ALU.add)
            v.drain()
            v.tensor_scalar(ov[0:1, 66:82], ov[0:1, 66:82], 1.0, float(BLK), ALU.add, ALU.mult)
            v.drain()
            v.scalar_tensor_tensor(tabf[0:1, MAXB + E:2 * MAXB], ov[0:1, 32:48], float(T), ov[0:1, 66:82], ALU.mult, ALU.add)
            v.drain()
            v.tensor_copy(tab[0:1, 0:2 * MAXB + 1], tabf[0:1, 0:2 * MAXB + 1])
            v.tensor_copy(bparts[0:32], braw)
            v.drain()
            v.tensor_tensor(bres, braw, bparts[0:32], ALU.subtract)
            v.drain()
            v.tensor_copy(bparts[32:64], bres)
            v.tensor_copy(bhalf, bres)
            v.drain()
            v.tensor_tensor(bres, bres, bhalf, ALU.subtract)
            v.drain()
            v.tensor_copy(bparts[64:96], bres)

        bhalf = work[0:32, 2048 + 6 * D:2048 + 6 * D + 3 * D // 2].bitcast(BF16)

        def h2_pool(g, key):
            g.nop().then_inc(S("h2_tile"), 1)
            with g.Fori(0, TT) as t:
                g.wait_ge(S("stage_ready"), t + 1 + before("stage_ready", key))
                g.dma_start(h2_dram[bass.ds(t * P, P), :], stage[:]).then_inc(S("h2_out"), 16)
                g.wait_ge(S("h2_out"), t * 16 + 16)
                g.nop().then_inc(S("h2_tile"), 1)

        UPC = (0, 2, 1, 3)
        xg = work[:, 0:1024]
        xgT = work[:, 1024:2048].rearrange("p (k n) -> p k n", k=KT)
        acts = work[:, 2048:3072]
        actT = work[:, 3072:4096].rearrange("p (k n) -> p k n", k=KT)
        ybuf = work[:, 4096:5120]
        gbuf = work[:, 5120:5632]
        lbuf = work[:, 5632:6144]
        sbuf_ = work[:, 6144:6656]
        idxA = sb("idxA", [P, 2], I32)
        idxB = sb("idxB", [P, 2], I32)
        ohb = sb("ohb", [96, P], BF16)
        WU = A["w_up"].rearrange("l e k n -> (l e) k n")
        WD = A["w_down"].rearrange("l e k n -> (l e) k n")

        def moe_w(e, s):
            if s < 4:
                return WU[bass.ds(e, 1), :, UPC[s] * CH:(UPC[s] + 1) * CH].rearrange("a (t p) n -> p (a t) n", p=P)
            return WD[bass.ds(e, 1), :, (s - 4) * CH:(s - 3) * CH].rearrange("a (t p) n -> p (a t) n", p=P)

        def blocks(eng):
            return eng.value_load(tab[0:1, 2 * MAXB:2 * MAXB + 1], min_val=E, max_val=MAXB - 1)

        def moe_sp_first(sp):
            for s in range(6):
                sp.wait_ge(freed[s], loads[s] + 1)
                sp.dma_start(slots[:, s], moe_w(0, s)).then_inc(landed[s], 16)

        def moe_sp(sp):
            nb = blocks(sp)
            with sp.Fori(1, nb) as b:
                e = sp.value_load(tab[0:1, bass.ds(b, 1)], min_val=0, max_val=E - 1)
                for s in range(6):
                    sp.wait_ge(freed[s], b + (loads[s] + 1))
                    sp.dma_start(slots[:, s], moe_w(e, s)).then_inc(landed[s], 16)

        tick = sb("tick", [1, 2])

        def settle(g):
            g.tensor_tensor(tick[:, 1:2], tick[:, 0:1], tick[:, 0:1], ALU.add)
            g.drain()

        def moe_list(g, at, n):
            row = g.value_load(tab[0:1, bass.ds(at, 1)] if not isinstance(at, int) else tab[0:1, at:at + 1], min_val=0, max_val=LROWS - P)
            g.dma_start(idxA[:], list_dram[bass.ds(row, P), :]).then_inc(S("idxA_in"), 16)
            g.wait_ge(S("idxA_in"), n * 16 + 16)

        def moe_gather(g, n):
            g.wait_ge(S("xg_free"), n + 1)
            settle(g)
            g.indirect_dma_start(xg, None, h2_dram, bass.IndirectOffsetOnAxis(ap=idxA[:, 0:1], axis=0)).then_inc(S("xg_in"), 16)

        def moe_pool(g):
            g.memset(tick[:], 0.0)
            g.drain()
            moe_list(g, MAXB, 0)
            moe_gather(g, 0)
            g.wait_ge(S("xg_in"), 16)
            settle(g)
            moe_list(g, MAXB + 1, 1)
            moe_gather(g, 1)
            nb = blocks(g)
            with g.Fori(0, nb) as b:
                g.wait_ge(S("xg_in"), b * 16 + 32)
                settle(g)
                moe_list(g, b + (MAXB + 2), b + 2)
                row = g.value_load(tab[0:1, bass.ds(b + MAXB, 1)], min_val=0, max_val=LROWS - P)
                g.dma_start(idxB[:], list_dram[bass.ds(row, P), :]).then_inc(S("idxB_in"), 16)
                g.wait_ge(S("idxB_in"), b * 16 + 16)
                g.wait_ge(S("y_ready"), b + 1)
                settle(g)
                g.indirect_dma_start(y_dram, bass.IndirectOffsetOnAxis(ap=idxB[:, 1:2], axis=0), ybuf, None,
                                     bounds_check=T * TOPK - 1, oob_is_err=False).then_inc(S("y_out"), 16)
                moe_gather(g, b + 2)
                g.wait_ge(S("y_out"), b * 16 + 16)
                settle(g)
                g.drain().then_inc(S("ybuf_free"), 1)

        def moe_pe(pe):
            pe.nop().then_inc(S("xg_free"), 1)
            pe.wait_ge(S("xg_in"), 16)
            for j in range(2):
                for k in range(4):
                    ins = pe.transpose(ps[:, 6 + j, k * P:(k + 1) * P], xg[:, (4 * j + k) * P:(4 * j + k + 1) * P], ident[:])
                ins.then_inc(S("moe_turned"), 1)
            pe.drain().then_inc(S("xg_free"), 1)
            nb = blocks(pe)
            with pe.Fori(0, nb) as b:
                def turn(j, src, half):
                    pe.wait_ge(S("moe_turned_out"), b * 4 + (j + 3))
                    for k in range(4):
                        ins = pe.transpose(ps[:, 6 + j % 2, k * P:(k + 1) * P], src[:, (4 * half + k) * P:(4 * half + k + 1) * P], ident[:])
                    return ins.then_inc(S("moe_turned"), 1)

                def down(ks):
                    for h in range(2):
                        for k in ks:
                            ins = pe.matmul(ps[:, 4 + h], actT[:, k], slots[:, 4 + h, k], start=k == 0, stop=False)
                        if ks[-1] == KT - 1:
                            pe.matmul(ps[:, 4 + h], ohb[:], bparts[:, 2 * D + h * CH:2 * D + (h + 1) * CH], start=False, stop=True)
                    return ins

                pe.wait_ge(S("moe_turned_out"), b * 4 + 4)
                for s in range(4):
                    pe.wait_ge(landed[s], b * 16 + (16 * uses[s] + 16))
                    pe.wait_ge(S("up_free"), b * 2 + (s // 2 + 1))
                    for k in range(KT):
                        ins = pe.matmul(ps[:, s], xgT[:, k], slots[:, s, k], start=k == 0, stop=False)
                    ins.then_inc(freed[s], 1)
                    if s == 0:
                        pe.wait_ge(S("ohb_ready"), b + 1)
                    pe.matmul(ps[:, s], ohb[:], bparts[:, UPC[s] * CH:(UPC[s] + 1) * CH], start=False, stop=True).then_inc(S("up_ready"), 1)
                pe.wait_ge(S("act_ready"), b * 2 + 1)
                turn(0, acts, 0)
                pe.wait_ge(S("xg_in"), b * 16 + 32)
                turn(1, xg, 0)
                pe.wait_ge(S("moe_turned_out"), b * 4 + 5)
                pe.wait_ge(landed[4], b * 16 + (16 * uses[4] + 16))
                pe.wait_ge(landed[5], b * 16 + (16 * uses[5] + 16))
                pe.wait_ge(S("down_free"), b + 1)
                down(range(4))
                pe.wait_ge(S("act_ready"), b * 2 + 2)
                turn(2, acts, 1)
                turn(3, xg, 1)
                pe.drain().then_inc(S("xg_free"), 1)
                pe.wait_ge(S("moe_turned_out"), b * 4 + 7)
                down(range(4, 8))
                pe.drain().then_inc(S("down_ready"), 1)
                pe.drain().then_inc(freed[4], 1)
                pe.drain().then_inc(freed[5], 1)

        def moe_act(a):
            a.nop().then_inc(S("moe_turned_out"), 2)
            for j in range(2):
                a.wait_ge(S("moe_turned"), j + 1)
                a.copy(xgT[:, 4 * j:4 * j + 4].rearrange("p k n -> p (k n)"), ps[:, 6 + j]).then_inc(S("moe_turned_out"), 1)
            nb = blocks(a)
            with a.Fori(0, nb) as b:
                def out(j, dst, half):
                    a.wait_ge(S("moe_turned"), b * 4 + (j + 3))
                    a.copy(dst[:, 4 * half:4 * half + 4].rearrange("p k n -> p (k n)"), ps[:, 6 + j % 2]).then_inc(S("moe_turned_out"), 1)

                def sig(h):
                    a.wait_ge(S("g_clipped"), b * 2 + (h + 1))
                    a.activation(sbuf_, gbuf, ACT.Sigmoid, scale=ALPHA).then_inc(S("sig_ready"), 1)

                sig(0)
                out(0, actT, 0)
                out(1, xgT, 0)
                sig(1)
                out(2, actT, 1)
                out(3, xgT, 1)

        def moe_dve(v):
            v.nop().then_inc(S("up_free"), 2)
            v.nop().then_inc(S("down_free"), 1)
            v.nop().then_inc(S("ybuf_free"), 1)
            nb = blocks(v)
            with v.Fori(0, nb) as b:
                v.tensor_copy(ohb[:], ohE[:, bass.ds(b, 1)].broadcast_to([96, P])).then_inc(S("ohb_ready"), 1)
                for h in range(2):
                    v.wait_ge(S("up_ready"), b * 4 + (2 * h + 2))
                    v.tensor_scalar(gbuf, ps[:, 2 * h], LIMIT, None, ALU.min).then_inc(S("g_clipped"), 1)
                    v.tensor_scalar(lbuf, ps[:, 2 * h + 1], -LIMIT, LIMIT, ALU.max, ALU.min).then_inc(S("up_free"), 1)
                    v.wait_ge(S("sig_ready"), b * 2 + (h + 1))
                    v.tensor_tensor(gbuf, gbuf, sbuf_, ALU.mult)
                    v.drain()
                    v.scalar_tensor_tensor(acts[:, h * CH:(h + 1) * CH], lbuf, 1.0, gbuf, ALU.add, ALU.mult).then_inc(S("act_ready"), 1)
                    v.drain()
                v.wait_ge(S("down_ready"), b + 1)
                v.wait_ge(S("ybuf_free"), b + 1)
                v.tensor_copy(ybuf.rearrange("p (h n) -> p h n", h=2), ps[:, 4:6]).then_inc(S("y_ready"), 1)
                v.drain().then_inc(S("down_free"), 1)

        ycomb = work[:, 0:8192].rearrange("p (b j n) -> p b j n", b=2, j=TOPK)

        def comb_loads(sp):
            yv = y_dram.rearrange("(t p j) n -> t p j n", p=P, j=TOPK)
            for t in range(TT):
                if t >= 1:
                    sp.wait_ge(S("comb_in"), t * 16)
                if t >= 2:
                    sp.wait_ge(S("comb_used"), t - 1)
                sp.dma_start(ycomb[:, t % 2], yv[t]).then_inc(S("comb_in"), 16)

        def comb_dve(v):
            for t in range(TT):
                v.wait_ge(S("comb_in"), t * 16 + 16)
                yt = ycomb[:, t % 2]
                v.tensor_scalar(stage[:], yt[:, 0], gates[:, 4 * t:4 * t + 1], None, ALU.mult)
                for j in range(1, TOPK):
                    v.drain()
                    ins = v.scalar_tensor_tensor(stage[:], yt[:, j], gates[:, 4 * t + j:4 * t + j + 1], stage[:], ALU.mult, ALU.add)
                ins.then_inc(S("comb_used"), 1)
                v.drain()
                v.tensor_tensor(stage[:], stage[:], modG[:], ALU.mult)
                v.drain()
                v.tensor_tensor(X[:, t], X[:, t], stage[:], ALU.add)
                v.drain()

        Y = work[:, 9216:13312].rearrange("p (t n) -> p t n", t=TT)

        def ln_loads(sp, key, i, s):
            sp.dma_start(tmp[:], A["ln_g_2"][i, s:s + 1].broadcast_to([P, D])).then_inc(S("ln_in"), 16)
            sp.dma_start(modB[:], A["ln_b_2"][i, s:s + 1].broadcast_to([P, D])).then_inc(S("ln_in"), 16)

        def ln_dve(v, key):
            neg_mu, var, rs = small[:, 0:4], small[:, 4:8], small[:, 8:12]
            n = TT * "abcd".index(key)
            v.tensor_scalar(modG[:], modG[:], 1.0, None, ALU.add)
            v.drain()
            for t in range(TT):
                v.tensor_tensor(Y[:, t], Y[:, t], modG[:], ALU.mult)
                v.drain()
                v.scalar_tensor_tensor(X[:, t], X[:, t], DN_ALPHA, Y[:, t], ALU.mult, ALU.add).then_inc(S("ln_sum"), 1)
            v.wait_ge(S("ln_squares"), n + TT)
            v.tensor_scalar(var, var, 1.0 / D, LN_EPS, ALU.mult, ALU.add).then_inc(S("var"), 1)
            v.wait_ge(S("sd"), before("sd", key) + 1)
            v.reciprocal(rs, rs)
            v.wait_ge(S("ln_in"), before("ln_in", key) + 32)
            v.drain()
            for t in range(TT):
                v.scalar_tensor_tensor(X[:, t], X[:, t], neg_mu[:, t:t + 1], tmp[:], ALU.add, ALU.mult)
                v.drain()
                v.scalar_tensor_tensor(X[:, t], X[:, t], rs[:, t:t + 1], modB[:], ALU.mult, ALU.add)

        def ln_act(a, key):
            neg_mu, var = small[:, 0:4], small[:, 4:8]
            n = TT * "abcd".index(key)
            for t in range(TT):
                a.wait_ge(S("ln_sum"), n + t + 1)
                a.drain()
                a.activation(stage[:], X[:, t], ACT.Identity, scale=-1.0 / D, accum_out=neg_mu[:, t:t + 1])
                a.drain()
                a.activation(stage[:], X[:, t], ACT.Square, bias=neg_mu[:, t:t + 1], accum_out=var[:, t:t + 1]).then_inc(S("ln_squares"), 1)
            a.wait_ge(S("var"), before("var", key) + 1)
            a.activation(small[:, 8:12], small[:, 4:8], ACT.Sqrt).then_inc(S("sd"), 1)

        landed2 = [S(f"landed_b{i}") for i in range(6)]
        freed2 = [S(f"freed_b{i}") for i in range(6)]

        def second(eng):
            landed[:] = landed2
            freed[:] = freed2

        qtok = work[:, 0:6144].rearrange("p (t n) -> p t n", t=TT)
        kTa = work[:, 6144:7680].rearrange("p (g n) -> p g n", g=KH)
        qTb = work[:, 7680:8704].rearrange("p (h n) -> p h n", h=QH)
        glog = work[:, 8704:10240].rearrange("p (h n) -> p h n", h=QK)
        gpT = work[:, 10240:11776].rearrange("p (j n) -> p j n", j=12)
        gqb = work[:, 11776:13312].rearrange("p (t n) -> p t n", t=TT)
        rope = modA[:, 0:TT * ROT].rearrange("p (t b n) -> p t b n", t=TT, b=2)
        rt = tmp[:, 0:640].rearrange("p (b h n) -> p b h n", b=4, h=10)
        vpad = scratch[:, 4096:5632].rearrange("p (b n) -> p b n", b=6)

        def at_loads(sp):
            sp.dma_start(rope, A["k_rope"].rearrange("p (t b n) -> p t b n", t=TT, b=2)).then_inc(S("at_in"), 16)
            sp.dma_start(gqb, A["k_gqbias"].rearrange("p (t n) -> p t n", t=TT)).then_inc(S("at_in"), 16)

        def at_pe(pe):
            for s in range(3):
                take(pe, s)
                for t in range(TT):
                    pe.wait_ge(S("bank_free"), before("bank_free", "at") + s * TT + t + 1)
                    for k in range(KT):
                        ins = pe.matmul(ps[:, t], hT[:, k, t * P:(t + 1) * P], slots[:, s, k], start=k == 0, stop=k == KT - 1)
                    ins.then_inc(S("product"), 1)
                pe.drain().then_inc(freed[s], 1)
            pe.wait_ge(S("roped"), 1)
            for g in range(KH):
                for t in range(TT):
                    ins = pe.transpose(ps[:, 4 + g, t * P:(t + 1) * P], qtok[:, t, QH * HD + g * HD:QH * HD + (g + 1) * HD], ident[:])
            ins.then_inc(S("k_turned"), 1)
            with pe.Fori(0, TT) as t:
                pe.wait_ge(S("att_normed"), t + (TT + 1))
                for h in range(QH):
                    ins = pe.transpose(ps[:, 6 + h // 4, (h % 4) * P:(h % 4 + 1) * P], stage[:, h * HD:(h + 1) * HD], ident[:])
                ins.then_inc(S("att_turned"), 1)
                pe.wait_ge(S("att_qk_ready"), t + (TT + 1))
                for g in range(KH):
                    if g:
                        pe.wait_ge(S("att_shifted"), t * 2 + (g + TT))
                    for j in range(QK):
                        ins = pe.matmul(ps[:, j, 0:3 * P], qTb[:, g * QK + j], kTa[:, g, bass.ds(t * P, 3 * P)], start=True, stop=True)
                    ins.then_inc(S("att_scores"), 1)
                for g in range(KH):
                    pe.wait_ge(S("att_exp"), t * 2 + (g + 1 + TT))
                    for j in range(12):
                        ins = pe.transpose(ps[:, 4 + j // 4, (j % 4) * P:(j % 4 + 1) * P], glogs[g][:, j // 3, (j % 3) * P:(j % 3 + 1) * P], ident[:])
                    ins.then_inc(S("att_pturned"), 1)
                    pe.wait_ge(S("att_pT"), t * 2 + (g + 1 + TT))
                    if g:
                        pe.wait_ge(S("att_tile_done"), t * 2 + (g + 1 + TT))
                    for j in range(QK):
                        for b in range(3):
                            ins = pe.matmul(ps[:, 7, j * P:(j + 1) * P], gpT[:, 3 * j + b], vpad[:, bass.ds(t + b, 1), g * HD:(g + 1) * HD], start=b == 0, stop=b == 2)
                    ins.then_inc(S("att_pv"), 1)
                pe.wait_ge(S("att_tile_done"), t * 2 + (3 + TT))

        def at_dve(v):
            v.nop().then_inc(S("bank_free"), 4)
            for s in range(3):
                for t in range(TT):
                    v.wait_ge(S("product"), before("product", "at") + s * TT + t + 1)
                    v.tensor_copy(qtok[:, t, s * CH:(s + 1) * CH], ps[:, t]).then_inc(S("bank_free"), 1)
            v.wait_ge(S("at_in"), 32)
            v.memset(kTa, 0.0)
            v.drain()
            H = ROT // 2
            for t in range(TT):
                q = qtok[:, t, 0:1280].rearrange("p (h d) -> p h d", d=HD)
                q1, q2 = q[:, :, 0:H], q[:, :, H:ROT]
                cs = rope[:, t, 0:1].broadcast_to([P, 10, H])
                sn = rope[:, t, 1:2].broadcast_to([P, 10, H])
                v.tensor_tensor(rt[:, 0], q1, cs, ALU.mult)
                v.tensor_tensor(rt[:, 1], q2, sn, ALU.mult)
                v.tensor_tensor(rt[:, 2], q2, cs, ALU.mult)
                v.tensor_tensor(rt[:, 3], q1, sn, ALU.mult)
                v.drain()
                v.tensor_tensor(q1, rt[:, 0], rt[:, 1], ALU.subtract)
                v.tensor_tensor(q2, rt[:, 2], rt[:, 3], ALU.add)
                v.drain()
            v.drain().then_inc(S("roped"), 1)
            v.wait_ge(S("k_turned"), 1)
            v.tensor_copy(kTa[:, :, P:P + T], ps[:, 4:6])
            v.memset(vpad[:, 0], 0.0)
            v.memset(vpad[:, 5], 0.0)
            v.tensor_copy(vpad[:, 1:5], qtok[:, :, 1280:1536])
            v.drain()
            with v.Fori(0, TT) as t:
                v.tensor_copy(stage[:], qtok[:, t, 0:D]).then_inc(S("att_normed"), 1)
                v.wait_ge(S("att_turned"), t + (TT + 1))
                v.tensor_copy(qTb.rearrange("p (b h) n -> p b (h n)", b=2), ps[:, 6:8]).then_inc(S("att_qk_ready"), 1)
                for g in range(KH):
                    mx, sk, nm = (small[:, 16 * g + 4 * j:16 * g + 4 * j + 4] for j in (0, 1, 3))
                    snk = sinks[:, SH + g * QK:SH + (g + 1) * QK]
                    v.wait_ge(S("att_scores"), t * 2 + (g + 1 + TT))
                    v.scalar_tensor_tensor(glogs[g], ps[:, 0:4, 0:3 * P], HD ** -0.5, gqb[:, bass.ds(t, 1)].broadcast_to([P, QK, 3 * P]), ALU.mult, ALU.add)
                    v.drain()
                    v.tensor_reduce(mx, glogs[g], AX_X, ALU.max)
                    v.drain()
                    v.tensor_tensor(mx, mx, snk, ALU.max)
                    v.drain()
                    v.tensor_tensor(sk, snk, mx, ALU.subtract)
                    v.tensor_scalar(nm, mx, -1.0, None, ALU.mult)
                    v.drain().then_inc(S("att_shifted"), 1)
                for g in range(KH):
                    sk, sm = (small[:, 16 * g + 4 * j:16 * g + 4 * j + 4] for j in (1, 2))
                    v.wait_ge(S("att_exp"), t * 2 + (g + 1 + TT))
                    v.tensor_tensor(sm, sm, sk, ALU.add)
                    v.drain()
                    v.reciprocal(sm, sm)
                    v.drain()
                    v.wait_ge(S("att_pv"), t * 2 + (g + 1 + TT))
                    v.tensor_tensor(qtok[:, t, g * CH:(g + 1) * CH].rearrange("p (h d) -> p h d", h=QK), ps[:, 7].rearrange("p (h d) -> p h d", h=QK),
                                    sm.unsqueeze(2).broadcast_to([P, QK, HD]), ALU.mult).then_inc(S("att_tile_done"), 1)
                v.drain()

        glogs = [glog, hT[:].rearrange("p k t -> p (k t)")[:, 0:3 * CH].rearrange("p (h n) -> p h n", h=QK)]

        def at_act(a):
            with a.Fori(0, TT) as t:
                def exps(g):
                    a.wait_ge(S("att_shifted"), t * 2 + (g + 1 + TT))
                    for j in range(QK):
                        a.activation(glogs[g][:, j], glogs[g][:, j], ACT.Exp, bias=small[:, 16 * g + 12 + j:16 * g + 13 + j],
                                     accum_out=small[:, 16 * g + 8 + j:16 * g + 9 + j])
                    a.activation(small[:, 16 * g + 4:16 * g + 8], small[:, 16 * g + 4:16 * g + 8], ACT.Exp).then_inc(S("att_exp"), 1)

                def probs_out(g):
                    a.wait_ge(S("att_pturned"), t * 2 + (g + 1 + TT))
                    a.copy(gpT.rearrange("p (b j) n -> p b (j n)", b=3), ps[:, 4:7]).then_inc(S("att_pT"), 1)

                exps(0)
                exps(1)
                probs_out(0)
                probs_out(1)

        def pair_dve_store(v, key):
            v.nop().then_inc(S("bank_free"), TT)
            for h in range(2):
                for t in range(TT):
                    v.wait_ge(S("product"), before("product", key) + h * TT + t + 1)
                    v.tensor_copy(Y[:, t, h * CH:(h + 1) * CH], ps[:, t]).then_inc(S("bank_free"), 1)

        h1T = work[:, 0:4096].rearrange("p (m n) -> p m n", m=8)
        NB = 4

        def mlp_sp(sp, i):
            w1, w2 = A["mlp_w1_2"][i], A["mlp_w2_2"][i]
            with sp.Fori(0, NB) as b:
                for s in range(2):
                    sp.wait_ge(freed[s], b + (loads[s] + 1))
                    sp.dma_start(slots[:, s], wview(w1[:, bass.ds(b * 2 * CH + s * CH, CH)])).then_inc(landed[s], 16)
                for s in range(2):
                    sp.wait_ge(freed[2 + s], b + (loads[2 + s] + 1))
                    sp.dma_start(slots[:, 2 + s], wview(w2[bass.ds(b * D, D), s * CH:(s + 1) * CH])).then_inc(landed[2 + s], 16)
            for s in range(4):
                loads[s] += NB

        def mlp_pe(pe, key):
            with pe.Fori(0, NB) as b:
                for s in range(2):
                    pe.wait_ge(landed[s], b * 16 + (16 * uses[s] + 16))
                    for m in range(4):
                        pe.wait_ge(S("hid_free"), b * 8 + (s * 4 + m + 1) + before("hid_free", key))
                        for k in range(KT):
                            ins = pe.matmul(ps[:, m], slots[:, s, k, m * P:(m + 1) * P], hT[:, k, :], start=k == 0, stop=k == KT - 1)
                        ins.then_inc(S("hid"), 1)
                    pe.drain().then_inc(freed[s], 1)
                pe.wait_ge(S("hid_sq"), b * 8 + 8 + before("hid_sq", key))
                for s in range(2):
                    pe.wait_ge(landed[2 + s], b * 16 + (16 * uses[2 + s] + 16))
                    for t in range(TT):
                        pe.wait_ge(S("out_free"), b * 8 + (s * 4 + t + 1) + before("out_free", key))
                        for k in range(KT):
                            ins = pe.matmul(ps[:, 4 + t], h1T[:, k, t * P:(t + 1) * P], slots[:, 2 + s, k], start=k == 0, stop=k == KT - 1)
                        ins.then_inc(S("outp"), 1)
                    pe.drain().then_inc(freed[2 + s], 1)
            for s in range(4):
                uses[s] += NB

        def mlp_act(a, key):
            a.nop().then_inc(S("hid_free"), 4)
            with a.Fori(0, NB) as b:
                for j in range(8):
                    a.wait_ge(S("hid"), b * 8 + (j + 1) + before("hid", key))
                    a.wait_ge(S("relu_free"), b * 8 + (j + 1) + before("relu_free", key))
                    a.activation(stage[:, (j % 2) * CH:(j % 2 + 1) * CH], ps[:, j % 4], ACT.Relu).then_inc(S("hid_free"), 1)

        def mlp_dve(v, key):
            v.memset(Y[:], 0.0)
            v.nop().then_inc(S("relu_free"), 2)
            v.nop().then_inc(S("out_free"), 4)
            v.drain()
            with v.Fori(0, NB) as b:
                for j in range(8):
                    r = stage[:, (j % 2) * CH:(j % 2 + 1) * CH]
                    v.wait_ge(S("hid_free"), b * 8 + (j + 5) + before("hid_free", key))
                    if j == 0:
                        v.wait_ge(S("out_free"), b * 8 + 4 + before("out_free", key))
                    v.tensor_tensor(h1T[:, j], r, r, ALU.mult).then_inc(S("hid_sq"), 1)
                    v.drain().then_inc(S("relu_free"), 1)
                for s in range(2):
                    for t in range(TT):
                        v.wait_ge(S("outp"), b * 8 + (s * 4 + t + 1) + before("outp", key))
                        yv = Y[:, t, s * CH:(s + 1) * CH]
                        v.tensor_tensor(yv, yv, ps[:, 4 + t], ALU.add).then_inc(S("out_free"), 1)
                v.drain()

        xr = work[0:RW, 0:8192].rearrange("p (n t) -> p n t", n=RB)
        uu, aa = stage[0:RW, 0:CH], stage[0:RW, CH:2 * CH]
        rr, bb = tmp[0:RW, 0:CH], tmp[0:RW, CH:2 * CH]
        hf, hb = modA[0:RW, 0:CH], modA[0:RW, CH:2 * CH]
        wg = work[0:RW, 8192:8192 + 3072].rearrange("p (j n) -> p j n", n=RW)
        rp = modB[0:RW, 0:RB * 12]
        rcw = rp[:, 0:64].rearrange("p (w n) -> p w n", w=4)
        rcb = rp[:, 64:80]
        rba = rp[:, 80:112].rearrange("p (d n) -> p d n", d=2)
        rbx = rp[:, 112:144].rearrange("p (d n) -> p d n", d=2)
        lam = rp[:, 144:176].rearrange("p (d n) -> p d n", d=2)

        def bv(a):
            return a.rearrange("a (n p) -> p (a n)", p=RW)

        def rnn_small(sp):
            for w in range(4):
                sp.dma_start(rcw[:, w], bv(A["rnn_conv_w_2"][0, w:w + 1])).then_inc(S("rnn_in"), 16)
            sp.dma_start(rcb, bv(A["rnn_conv_b_2"])).then_inc(S("rnn_in"), 16)
            for d in range(2):
                for dst, name in ((rba, "rnn_b_a_2"), (rbx, "rnn_b_x_2"), (lam, "rnn_lam_2")):
                    sp.dma_start(dst[:, d], bv(A[name][0, d:d + 1])).then_inc(S("rnn_in"), 16)

        def rnn_w_half(sp, h):
            W = A["rnn_w_in_2"][0]
            for s in range(4):
                c = h * RW * RB + s * 4 * RW
                load(sp, s, wview(W[:, c:c + 4 * RW]), slots[:, s, :, 0:4 * RW])

        def rnn_w_out(sp, h, s0, reach=None):
            WO = A["rnn_w_out_2"][0].rearrange("(n p) c -> p n c", p=RW)
            for q in range(2):
                if q and reach:
                    reached(sp, reach)
                load(sp, s0 + q, WO[:, q * 8:(q + 1) * 8, h * CH:(h + 1) * CH], slots[0:RW, s0 + q])

        def rnn_gate_loads(sp, d):
            if d:
                sp.wait_ge(S("wg_free"), 1)
            for j, name in enumerate(("rnn_w_a_2", "rnn_w_x_2")):
                sp.dma_start(wg[:, j * RB:(j + 1) * RB], A[name][0, d].rearrange("n i j -> i n j")).then_inc(S("wg_in"), 16)

        NRIN = 11 * 16
        ysA = hT[0:RW].rearrange("p k t -> p (k t)").rearrange("p (n t) -> p n t", n=8)
        ysB = scratch[0:RW, 0:4096].rearrange("p (n t) -> p n t", n=8)

        def ys(n):
            return ysA[:, n] if n < 8 else ysB[:, n - 8]

        def rnn_pe(pe):
            for h in range(2):
                for s in range(4):
                    take(pe, s)
                    for m in range(4):
                        j = h * 16 + s * 4 + m
                        if j < RB + 4:
                            pe.wait_ge(S("bank_free"), before("bank_free", "r") + j + 1)
                        else:
                            pe.wait_ge(S("z_read"), TT + j - (RB + 4) + 1)
                        for k in range(KT):
                            ins = pe.matmul(ps[0:RW, m], slots[:, s, k, m * RW:(m + 1) * RW], hT[:, k, :], start=k == 0, stop=k == KT - 1)
                        ins.then_inc(S("product"), 1)
                    pe.drain().then_inc(freed[s], 1)

        def rnn_dve(v):
            v.wait_ge(S("rnn_in"), NRIN)
            v.nop().then_inc(S("bank_free"), 4)
            for n in range(RB):
                u, y = ps[0:RW, n % 4], xr[:, n]
                v.wait_ge(S("product"), before("product", "r") + n + 1)
                v.tensor_scalar(y, u, rcw[:, 2, n:n + 1], rcb[:, n:n + 1], ALU.mult, ALU.add)
                v.drain()
                v.scalar_tensor_tensor(y[:, 2:], u[:, 0:T - 2], rcw[:, 0, n:n + 1], y[:, 2:], ALU.mult, ALU.add)
                v.drain()
                v.scalar_tensor_tensor(y[:, 1:], u[:, 0:T - 1], rcw[:, 1, n:n + 1], y[:, 1:], ALU.mult, ALU.add)
                v.drain()
                v.scalar_tensor_tensor(y[:, 0:T - 1], u[:, 1:T], rcw[:, 3, n:n + 1], y[:, 0:T - 1], ALU.mult, ALU.add).then_inc(S("bank_free"), 1)

        gate_dram = dram("gate_dram", (RB, RW, T))
        gst = stage[0:RW].rearrange("p (b n) -> p b n", b=2)

        def rnn_act(a):
            for n in range(RB):
                a.wait_ge(S("product"), before("product", "r") + 16 + n + 1)
                if n >= 1:
                    a.wait_ge(S("gate_out"), n * 16)
                a.activation(gst[:, n % 2], ps[0:RW, n % 4], ACT.Gelu_apprx_tanh).then_inc(S("z_read"), 1)
                a.drain()
                a.dma_start(gate_dram[n], gst[:, n % 2]).then_inc(S("gate_out"), 16)
            a.wait_ge(S("gate_out"), RB * 16)

        BB = 4
        NBAT = 2 * RB // BB

        def four(a):
            return a[0:RW].rearrange("p (m t) -> p m t", m=BB)

        flat = [slots[:, i].rearrange("p k n -> p (k n)") for i in range(6)]
        decays = [four(flat[0][:, 0:2048]), four(flat[1][:, 0:2048]), four(flat[5][:, 0:2048])]
        inputs = [four(flat[0][:, 2048:4096]), four(flat[1][:, 2048:4096]), four(flat[5][:, 2048:4096])]
        mults = [four(flat[3][:, 0:2048]), four(flat[3][:, 2048:4096]), four(work[:, 11264:13312])]
        squares = [stage[0:RW, 0:CH], stage[0:RW, CH:2 * CH], tmp[0:RW, 0:CH], tmp[0:RW, CH:2 * CH]]

        def rnn2_pe(pe):
            for k in range(NBAT):
                d, n0 = k * BB // RB, k * BB % RB
                if n0 == 0:
                    pe.wait_ge(S("wg_in"), (d + 1) * 32)
                for m in range(BB):
                    if k:
                        pe.wait_ge(S("gate_read"), (k - 1) * BB + m + 1)
                    pe.matmul(ps[0:RW, m], wg[:, n0 + m], xr[:, n0 + m], start=True, stop=True)
                    pe.matmul(ps[0:RW, BB + m], wg[:, RB + n0 + m], xr[:, n0 + m], start=True, stop=True).then_inc(S("gate_ps"), 1)
                if n0 == RB - BB:
                    pe.drain().then_inc(S("wg_free"), 1)

        def rnn2_act(a):
            a.wait_ge(S("lam_abs"), 1)
            a.activation(lexp, lexp, ACT.Exp, scale=-1.0)
            a.drain()
            a.activation(lexp, lexp, ACT.Ln, bias=1.0).then_inc(S("lam_ln"), 1)
            a.wait_ge(S("lam_abs"), 2)

            def front(k):
                d, n0 = k * BB // RB, k * BB % RB
                A_, U_, M_ = decays[k % 3], inputs[k % 3], mults[k % 3]
                if k >= 3:
                    a.wait_ge(S("scan_done"), k - 2)
                for m in range(BB):
                    n = n0 + m
                    a.wait_ge(S("gate_ps"), k * BB + m + 1)
                    a.activation(A_[:, m], ps[0:RW, m], ACT.Sigmoid, bias=rba[:, d, n:n + 1])
                    a.activation(U_[:, m], ps[0:RW, BB + m], ACT.Sigmoid, bias=rbx[:, d, n:n + 1]).then_inc(S("gate_read"), 1)
                a.drain()
                for m in range(BB):
                    n = n0 + m
                    a.activation(M_[:, m], A_[:, m], ACT.Tanh, scale=lamn[:, d, n:n + 1])
                a.drain()
                for m in range(BB):
                    n = n0 + m
                    a.activation(A_[:, m], A_[:, m], ACT.Exp, scale=lam[:, d, n:n + 1]).then_inc(S("exp_tanh"), 1)

            for k in range(NBAT + 1):
                if k < NBAT:
                    front(k)
                if k:
                    a.wait_ge(S("one_m"), k)
                    a.activation(mults[(k - 1) % 3], mults[(k - 1) % 3], ACT.Sqrt).then_inc(S("mult_ready"), 1)

        lexp = hf[:, 0:32].rearrange("p (d n) -> p d n", d=2)
        lneg = hb[:, 0:32].rearrange("p (d n) -> p d n", d=2)
        lamn = rp[:, 0:32].rearrange("p (d n) -> p d n", d=2)

        def rnn2_pool(g):
            for k in range(NBAT):
                if k * BB == RB - BB:
                    rnn_gate_loads(g, 1)
                for m in range(BB):
                    g.wait_ge(S("exp_tanh"), k * BB + m + 1)
                    if k:
                        g.wait_ge(S("one_m"), k)
                    a_ = decays[k % 3][:, m]
                    g.tensor_tensor(squares[m], a_, a_, ALU.mult).then_inc(S("log_a"), 1)

        def rnn2_dve(v):
            v.tensor_scalar(lneg, lam, -1.0, None, ALU.mult)
            v.drain()
            v.tensor_tensor(lexp, lneg, lam, ALU.max).then_inc(S("lam_abs"), 1)
            v.wait_ge(S("lam_ln"), 1)
            v.scalar_tensor_tensor(lam, lneg, 0.0, lexp, ALU.max, ALU.add)
            v.drain()
            v.tensor_scalar(lamn, lam, LRU_C, None, ALU.mult)
            v.drain()
            v.tensor_scalar(lam, lamn, -1.0, None, ALU.mult).then_inc(S("lam_abs"), 1)

            def ends(k):
                d, n0 = k * BB // RB, k * BB % RB
                A_, U_, M_ = decays[k % 3], inputs[k % 3], mults[k % 3]
                v.wait_ge(S("mult_ready"), k + 1)
                v.tensor_tensor(U_, U_, M_, ALU.mult)
                v.drain()
                for m in range(BB):
                    if d == 0:
                        ins = v.tensor_tensor_scan(ys(n0 + m), A_[:, m], U_[:, m], 0.0, ALU.mult, ALU.add)
                    else:
                        ins = v.tensor_tensor_scan(M_[:, m, ::-1], A_[:, m, ::-1], U_[:, m, ::-1], 0.0, ALU.mult, ALU.add)
                v.drain()
                if d:
                    y4 = (ysA if n0 < 8 else ysB)[:, n0 % 8:n0 % 8 + BB]
                    v.tensor_tensor(y4, y4, M_, ALU.add)
                    v.drain()
                v.drain().then_inc(S("scan_done"), 1)

            for k in range(NBAT + 1):
                if k < NBAT:
                    n0 = k * BB % RB
                    A_, U_, M_ = decays[k % 3], inputs[k % 3], mults[k % 3]
                    v.wait_ge(S("gate_read"), (k + 1) * BB)
                    v.tensor_tensor(U_, U_, xr[:, n0:n0 + BB], ALU.mult)
                    for m in range(BB):
                        v.wait_ge(S("log_a"), k * BB + m + 1)
                        v.scalar_tensor_tensor(M_[:, m], squares[m], 1.0, M_[:, m], ALU.add, ALU.mult)
                    v.drain().then_inc(S("one_m"), 1)
                if k:
                    ends(k - 1)

        gin = stage[0:RW].rearrange("p (b n) -> p b n", b=2)

        def rnn3_loads(sp):
            for n in range(RB):
                if n >= 1:
                    sp.wait_ge(S("gate_back"), n * 16)
                if n >= 2:
                    sp.wait_ge(S("gated"), n - 1)
                sp.dma_start(gin[:, n % 2], gate_dram[n]).then_inc(S("gate_back"), 16)

        def rnn3_dve(v):
            for n in range(RB):
                v.wait_ge(S("gate_back"), n * 16 + 16)
                v.tensor_tensor(xr[:, n], ys(n), gin[:, n % 2], ALU.mult).then_inc(S("gated"), 1)
            v.nop().then_inc(S("bank_free"), TT)
            for h in range(2):
                for t in range(TT):
                    v.wait_ge(S("product"), before("product", "_ro") + h * TT + t + 1)
                    v.tensor_copy(Y[:, t, h * CH:(h + 1) * CH], ps[:, t]).then_inc(S("bank_free"), 1)

        def rnn3_pe(pe):
            pe.wait_ge(S("gated"), RB)
            for h in range(2):
                s0 = (4, 0)[h]
                take(pe, s0)
                take(pe, s0 + 1)
                for t in range(TT):
                    pe.wait_ge(S("bank_free"), before("bank_free", "_ro") + h * TT + t + 1)
                    for n in range(RB):
                        ins = pe.matmul(ps[:, t], xr[:, n, t * P:(t + 1) * P], slots[0:RW, s0 + n // 8, n % 8], start=n == 0, stop=n == RB - 1)
                    ins.then_inc(S("product"), 1)
                pe.drain().then_inc(freed[s0], 1)
                pe.drain().then_inc(freed[s0 + 1], 1)

        def out_sp(sp):
            ov_ = out.rearrange("a (t p) d -> p (a t) d", p=P)
            sp.dma_start(ov_, X[:]).then_inc(S("written"), 16)
            sp.wait_ge(S("written"), 16)

        STAGES = {}

        def reached(sp, n):
            sp.wait_ge(S("stage_done"), 4 * n)

        A2 = 6 * D

        def mods(l, s):
            at = A2 + (2 * l + s) * 3 * D
            return at + D, at, at + 2 * D

        with nc.Block() as block:
            @block.sync
            def _(sp):
                sp_constants(sp)
                ada_sp(sp)
                proj_sp(sp)
                pair_sp(sp, A["w_out"][0], 0)
                reached(sp, 7)
                moe_sp_first(sp)
                reached(sp, 10)
                moe_sp(sp)
                second(sp)
                for s in range(6):
                    loads[s] = 0
                for s in range(3):
                    load(sp, s, wview(A["attn_w_in_2"][0][:, s * CH:(s + 1) * CH]))
                pair_sp(sp, A["attn_w_out_2"][0], 4)
                reached(sp, 14)
                mlp_sp(sp, 0)
                rnn_w_half(sp, 0)
                rnn_w_half(sp, 1)
                rnn_w_out(sp, 0, 4, reach=22)
                rnn_w_out(sp, 1, 0)
                reached(sp, 23)
                mlp_sp(sp, 1)
                reached(sp, 27)
                out_sp(sp)

            def first_slots():
                landed[:] = [S(f"landed{i}") for i in range(6)]
                freed[:] = [S(f"freed{i}") for i in range(6)]

            @block.tensor
            def _(pe):
                def end():
                    meet(pe, "pe")
                first_slots()
                ada_pe(pe)
                for s in range(6):
                    uses[s] = 6
                end()
                turn_pe(pe, "1"); end()
                proj_pe(pe); end()
                dn1_pe(pe); end()
                dn2_pe(pe); end()
                end()
                sw_pe(pe)
                turn_pe(pe, "w"); end()
                pair_pe(pe, "w", 0); end()
                turn_pe(pe, "2"); end()
                route_pe(pe); end()
                moe_pe(pe)
                second(pe)
                for s in range(6):
                    uses[s] = 0
                    pe.nop().then_inc(freed[s], 1)
                end()
                end()
                turn_pe(pe, "3", 2); end()
                at_pe(pe)
                turn_pe(pe, "o"); end()
                pair_pe(pe, "o", 4); end()
                end()
                turn_pe(pe, "4", 2); end()
                mlp_pe(pe, "m0"); end()
                end()
                turn_pe(pe, "5", 2); end()
                rnn_pe(pe); end()
                rnn2_pe(pe); end()
                rnn3_pe(pe); end()
                end()
                turn_pe(pe, "6", 2); end()
                mlp_pe(pe, "m1"); end()
                end()

            @block.vector
            def _(v):
                def end():
                    meet(v, "dve")
                first_slots()
                ada_dve(v); end()
                norm_dve(v, "1", True); end()
                proj_dve(v); end()
                dn1_dve(v); end()
                dn2_dve(v); end()
                dn3_dve(v); end()
                sw_dve(v)
                v.drain()
                turn_tiles_dve(v, "w", mixed); end()
                pair_dve_residual(v, "w"); end()
                norm_dve(v, "2", True, store=True); end()
                route_dve(v); end()
                moe_dve(v); end()
                comb_dve(v); end()
                norm_dve(v, "3", False); end()
                at_dve(v)
                v.drain()
                turn_tiles_dve(v, "o", qtok[:, :, 0:D]); end()
                pair_dve_store(v, "o"); end()
                ln_dve(v, "a"); end()
                norm_dve(v, "4", False); end()
                mlp_dve(v, "m0"); end()
                ln_dve(v, "b"); end()
                norm_dve(v, "5", False); end()
                rnn_dve(v); end()
                rnn2_dve(v); end()
                rnn3_dve(v); end()
                ln_dve(v, "c"); end()
                norm_dve(v, "6", False); end()
                mlp_dve(v, "m1"); end()
                ln_dve(v, "d"); end()

            @block.scalar
            def _(a):
                def end():
                    meet(a, "act")
                first_slots()
                ada_act(a); end()
                rms_scales_act(a, "1"); turn_act(a, "1"); end()
                proj_act(a); end()
                dn1_act(a); end()
                dn2_act(a); end()
                dn3_act(a); end()
                sw_act(a)
                turn_act(a, "w"); end()
                end()
                rms_scales_act(a, "2"); turn_act(a, "2"); end()
                route_act(a); end()
                moe_act(a); end()
                end()
                turn_act(a, "3"); end()
                at_act(a)
                turn_act(a, "o"); end()
                end()
                ln_act(a, "a"); end()
                turn_act(a, "4"); end()
                mlp_act(a, "m0"); end()
                ln_act(a, "b"); end()
                turn_act(a, "5"); end()
                rnn_act(a); end()
                rnn2_act(a); end()
                end()
                ln_act(a, "c"); end()
                turn_act(a, "6"); end()
                mlp_act(a, "m1"); end()
                ln_act(a, "d"); end()

            @block.gpsimd
            def _(g):
                def end():
                    meet(g, "pool")
                ada_pool(g); end()
                mod_load(g, "1", D, 0, 2 * D, A["norm1_w"]); end()
                mixer_loads(g); end()
                dn1_pool(g); dn1_moves(g); end()
                end()
                sw_pool(g); end()
                end()
                route_fill(g); route_loads(g); end()
                mod_load(g, "2", 4 * D, 3 * D, 5 * D, A["norm2_w"]); h2_pool(g, "2"); end()
                route_pool(g); end()
                moe_pool(g); end()
                comb_loads(g); end()
                mod_load(g, "3", *mods(0, 0)); end()
                at_loads(g); end()
                ln_loads(g, "a", 0, 0); end()
                end()
                mod_load(g, "4", *mods(0, 1)); end()
                ln_loads(g, "b", 0, 1); end()
                end()
                mod_load(g, "5", *mods(1, 0)); end()
                rnn_small(g); rnn_gate_loads(g, 0); end()
                rnn2_pool(g); end()
                rnn3_loads(g); ln_loads(g, "c", 1, 0); end()
                end()
                mod_load(g, "6", *mods(1, 1)); end()
                ln_loads(g, "d", 1, 1); end()
                end()


_INS = ['x', 'c', 'w_ada', 'b_ada', 'norm1_w', 'w_in', 'conv_w', 'a_log', 'dt_bias', 'dn_norm_w', 'q_norm_w', 'k_norm_w',
        'sinks', 'w_out', 'norm2_w', 'w_router', 'b_router', 'w_up', 'b_up', 'w_down', 'b_down', 'c_2', 'ada_w_2',
        'ada_b_2', 'ln_g_2', 'ln_b_2', 'attn_w_in_2', 'attn_w_out_2', 'attn_sinks_2', 'rnn_w_in_2', 'rnn_conv_w_2',
        'rnn_conv_b_2', 'rnn_w_a_2', 'rnn_b_a_2', 'rnn_w_x_2', 'rnn_b_x_2', 'rnn_lam_2', 'rnn_w_out_2', 'mlp_w1_2',
        'mlp_w2_2']
_OUTS = [((1, 512, 1024), 'float32')]


def kernel(**inputs):
    import numpy as _np
    import concourse.bacc as _bacc
    from concourse import mybir as _mybir
    from concourse.bass_utils import run_bass_kernel_spmd as _run

    nc = _bacc.Bacc("TRN2", target_bir_lowering=False, num_devices=1)
    arrays, args = {}, {}
    given = {name: inputs[name] for name in _INS}
    given.update({"k_" + name: value for name, value in constants().items()})
    for name, value in given.items():
        a = _np.ascontiguousarray(value)
        arrays[f"in_{name}_dram"] = a
        args[name] = nc.dram_tensor(f"in_{name}_dram", a.shape, _mybir.dt.from_np(a.dtype), kind="ExternalInput").ap()
    outs = []
    for i, (shape, dtype) in enumerate(_OUTS):
        dt = _mybir.dt.from_np(_np.dtype(dtype))
        outs.append(nc.dram_tensor(f"out_{i}_dram", shape, dt, kind="ExternalOutput").ap())
    build(nc, args, outs[0])
    r = _run(nc, [arrays], core_ids=[0])
    return r.results[0]["out_0_dram"]
```
